# Optimizing a Trainium2 kernel written in Bass

```python
import math
import jax, jax.numpy as jnp
from jax import lax
import numpy as np

D_MODEL = 2048
BATCH = 1
SEQ = 256
DEPTH = 1

ATTN_HEADS = 16
HEAD_DIM = 128
ATTN_W = ATTN_HEADS * HEAD_DIM
DILATED_GROUPS = ((128, 1), (512, 4), (2048, 16))
BLK = 128
LRU_W = D_MODEL
LRU_HEADS = 16
LRU_BLK = LRU_W // LRU_HEADS
CONV_W = 4
LRU_C = 8.0
D_FF = 4 * D_MODEL
EPS = 1e-6
IN_SPLITS = (ATTN_W, ATTN_W, ATTN_W, LRU_W, LRU_W, D_MODEL, D_MODEL)
IN_COLS = sum(IN_SPLITS)

kernel_name = "hybrid_dilated_attn_rglru_gated_block"

def rms_norm(x, g):
    xf = x.astype(jnp.float32)
    y = xf * lax.rsqrt(jnp.mean(xf * xf, axis=-1, keepdims=True) + EPS)
    return (y * g.astype(jnp.float32)).astype(x.dtype)

def alibi_slopes(n_heads):
    return 2.0 ** (-8.0 * jnp.arange(1, n_heads + 1, dtype=jnp.float32) / n_heads)

def dilated_group_attention(q, k, v, slopes, window, dilation):
    b, s, h, dh = q.shape
    d = dilation
    span = window // d
    u_len = s // d
    n_blk = -(-u_len // BLK)
    u_pad = n_blk * BLK
    qs = q.reshape(b, u_len, d, h, dh)
    ks = k.reshape(b, u_len, d, h, dh)
    vs = v.reshape(b, u_len, d, h, dh)
    qb = jnp.pad(qs, ((0, 0), (0, u_pad - u_len), (0, 0), (0, 0), (0, 0))).reshape(b, n_blk, BLK, d, h, dh)
    pad_kv = ((0, 0), (BLK, u_pad - u_len), (0, 0), (0, 0), (0, 0))
    kp = jnp.pad(ks, pad_kv).reshape(b, n_blk + 1, BLK, d, h, dh)
    vp = jnp.pad(vs, pad_kv).reshape(b, n_blk + 1, BLK, d, h, dh)
    kwin = jnp.concatenate([kp[:, :-1], kp[:, 1:]], axis=2)
    vwin = jnp.concatenate([vp[:, :-1], vp[:, 1:]], axis=2)
    scores = jnp.einsum('bnqrhe,bnkrhe->bnrhqk', qb, kwin).astype(jnp.float32) * (HEAD_DIM ** -0.5)
    i = jnp.arange(BLK)[:, None]
    j = jnp.arange(2 * BLK)[None, :]
    diff = BLK + i - j
    band = (diff >= 0) & (diff <= span)
    n_idx = jnp.arange(n_blk)[:, None, None]
    valid = band[None] & ((n_idx - 1) * BLK + j[None] >= 0)
    bias = -(slopes * d)[:, None, None] * diff.astype(jnp.float32)[None]
    scores = scores + bias[None, None, None]
    scores = jnp.where(valid[None, :, None, None], scores, -jnp.inf)
    m = jnp.max(scores, axis=-1, keepdims=True)
    p = jnp.exp(scores - m)
    l = jnp.sum(p, axis=-1)
    o = jnp.einsum('bnrhqk,bnkrhe->bnqrhe', p.astype(v.dtype), vwin).astype(jnp.float32)
    l_t = jnp.transpose(l, (0, 1, 4, 2, 3))
    o = o / l_t[..., None]
    lse = jnp.transpose(m[..., 0] + jnp.log(l), (0, 1, 4, 2, 3))
    o = o.reshape(b, u_pad, d, h, dh)[:, :u_len].reshape(b, s, h, dh)
    lse = lse.reshape(b, u_pad, d, h)[:, :u_len].reshape(b, s, h)
    return o, lse

def dilated_attention(q, k, v):
    b, s, _ = q.shape
    q = q.reshape(b, s, ATTN_HEADS, HEAD_DIM)
    k = k.reshape(b, s, ATTN_HEADS, HEAD_DIM)
    v = v.reshape(b, s, ATTN_HEADS, HEAD_DIM)
    slopes = alibi_slopes(ATTN_HEADS)
    outs, lses = [], []
    for window, dilation in DILATED_GROUPS:
        o, lse = dilated_group_attention(q, k, v, slopes, window, dilation)
        outs.append(o)
        lses.append(lse)
    w = jax.nn.softmax(jnp.stack(lses, axis=0), axis=0)
    out = jnp.sum(w[..., None] * jnp.stack(outs, axis=0), axis=0)
    return out.reshape(b, s, ATTN_W).astype(q.dtype)

def rg_lru_branch(xr, gate, conv_w, conv_b, wa, ba, wx, bx, lam):
    b, s, c = xr.shape
    xc = lax.conv_general_dilated(
        xr, conv_w.reshape(CONV_W, 1, c).astype(xr.dtype), window_strides=(1,),
        padding=[(CONV_W - 1, 0)], dimension_numbers=('NWC', 'WIO', 'NWC'),
        feature_group_count=c) + conv_b
    xh = xc.reshape(b, s, LRU_HEADS, LRU_BLK)
    r = jax.nn.sigmoid((jnp.einsum('bshi,hij->bshj', xh, wa).reshape(b, s, c) + ba).astype(jnp.float32))
    ig = jax.nn.sigmoid((jnp.einsum('bshi,hij->bshj', xh, wx).reshape(b, s, c) + bx).astype(jnp.float32))
    log_a = -LRU_C * r * jax.nn.softplus(-lam.astype(jnp.float32))
    a = jnp.exp(log_a)
    mult = jnp.sqrt(-jnp.expm1(2.0 * log_a))
    u = mult * (ig * xc.astype(jnp.float32))

    def combine(c1, c2):
        a1, b1 = c1
        a2, b2 = c2
        return a1 * a2, a2 * b1 + b2

    _, hseq = lax.associative_scan(combine, (a, u), axis=1)
    return (hseq * jax.nn.gelu(gate.astype(jnp.float32))).astype(xr.dtype)

def setup_inputs(seed: int = 0) -> dict:
    key = jax.random.key(seed)
    ks = jax.random.split(key, 20)
    f32 = jnp.float32
    nrm = lambda k, shape, scale: jax.random.normal(k, shape, f32) * scale
    a8 = jax.random.uniform(ks[9], (DEPTH, LRU_W), f32, 0.9, 0.999)
    a_base = a8 ** (1.0 / LRU_C)
    lru_lambda = jnp.log(a_base) - jnp.log1p(-a_base)
    return {
        "x": jax.random.normal(ks[0], (BATCH, SEQ, D_MODEL), f32),
        "norm_mix_g": 1.0 + nrm(ks[1], (DEPTH, D_MODEL), 0.02),
        "w_in": nrm(ks[2], (DEPTH, D_MODEL, IN_COLS), D_MODEL ** -0.5),
        "conv_w": nrm(ks[3], (DEPTH, CONV_W, LRU_W), CONV_W ** -0.5),
        "conv_b": nrm(ks[4], (DEPTH, LRU_W), 0.02),
        "lru_wa": nrm(ks[5], (DEPTH, LRU_HEADS, LRU_BLK, LRU_BLK), LRU_BLK ** -0.5),
        "lru_ba": nrm(ks[6], (DEPTH, LRU_W), 0.02),
        "lru_wx": nrm(ks[7], (DEPTH, LRU_HEADS, LRU_BLK, LRU_BLK), LRU_BLK ** -0.5),
        "lru_bx": nrm(ks[8], (DEPTH, LRU_W), 0.02),
        "lru_lambda": lru_lambda,
        "w_proj_attn": nrm(ks[10], (DEPTH, ATTN_W, D_MODEL), ATTN_W ** -0.5),
        "w_proj_lru": nrm(ks[11], (DEPTH, LRU_W, D_MODEL), LRU_W ** -0.5),
        "w_out": nrm(ks[12], (DEPTH, D_MODEL, D_MODEL), D_MODEL ** -0.5),
        "norm_mlp_g": 1.0 + nrm(ks[13], (DEPTH, D_MODEL), 0.02),
        "w_up": nrm(ks[14], (DEPTH, D_MODEL, D_FF), D_MODEL ** -0.5),
        "w_down": nrm(ks[15], (DEPTH, D_FF, D_MODEL), D_FF ** -0.5),
        "norm_final_g": 1.0 + nrm(ks[16], (D_MODEL,), 0.02),
    }

def reference(x, norm_mix_g, w_in, conv_w, conv_b, lru_wa, lru_ba, lru_wx, lru_bx, lru_lambda,
              w_proj_attn, w_proj_lru, w_out, norm_mlp_g, w_up, w_down, norm_final_g):
    h = x
    split_idx = list(np.cumsum(IN_SPLITS)[:-1])
    for l in range(DEPTH):
        xn = rms_norm(h, norm_mix_g[l])
        proj = jnp.einsum('bsd,dc->bsc', xn, w_in[l])
        q, k, v, xr, xg, g_attn, g_lru = jnp.split(proj, split_idx, axis=-1)
        y_attn = dilated_attention(q, k, v)
        y_lru = rg_lru_branch(xr, xg, conv_w[l], conv_b[l], lru_wa[l], lru_ba[l],
                              lru_wx[l], lru_bx[l], lru_lambda[l])
        merged = (jax.nn.sigmoid(g_attn) * jnp.einsum('bsc,cd->bsd', y_attn, w_proj_attn[l])
                  + jax.nn.sigmoid(g_lru) * jnp.einsum('bsc,cd->bsd', y_lru, w_proj_lru[l]))
        h = h + jnp.einsum('bsd,de->bse', merged, w_out[l])
        hn = rms_norm(h, norm_mlp_g[l])
        hid = jnp.square(jax.nn.relu(jnp.einsum('bsd,df->bsf', hn, w_up[l])))
        h = h + jnp.einsum('bsf,fd->bsd', hid, w_down[l])
    return rms_norm(h, norm_final_g)


_drawn_inputs = setup_inputs


def setup_inputs(seed=0):
    import zlib

    import numpy as np

    out = dict(_drawn_inputs(seed))
    spreads = {}
    factors = {'norm_mix_g': 6.105,
     'lru_ba': 23.549,
     'lru_bx': 8.0,
     'norm_mlp_g': 10.848,
     'norm_final_g': 8.467,
     'conv_b': 3.692}
    for name, (base, spread) in spreads.items():
        noise = np.random.default_rng([zlib.crc32(name.encode()), seed]).standard_normal(out[name].shape)
        drawn = base * np.exp(spread * noise) if base else spread * noise
        out[name] = __import__('jax').numpy.asarray(drawn.astype(out[name].dtype))
    for name, factor in factors.items():
        out[name] = (out[name] * factor).astype(out[name].dtype)
    return out
```

```python
from contextlib import ExitStack

import concourse.bass as bass
from concourse import mybir

F32 = mybir.dt.float32
F32R = mybir.dt.float32r
I32 = mybir.dt.int32
ALU = mybir.AluOpType
ACT = mybir.ActivationFunctionType
AX_X = mybir.AxisListType.X
ds = bass.ds

P = 128
SEQ = 256
TB = SEQ // P
D = 2048
KT = D // P
NC = 512
COLS = D // NC
HC = NC // P
CHUNKS = 8
CK = KT // CHUNKS
RING = 4
AHEAD = RING
F = 4 * D
GROUPS = F // D
CONV_W = 4
PAD = CONV_W - 1
HEADS = 16
QK_SCALE = float(P) ** -0.5
LRU_C = 8.0
EPS = 1e-6
MASKED = -1e30

U_LRU = 0
U_PLRU = U_LRU + 3 * COLS
U_ATT = U_PLRU + COLS
U_PATT = U_ATT + 4 * COLS
U_OUT = U_PATT + COLS
U_MLP = U_OUT + COLS

T_X = 0
T_LRU = T_X + COLS
T_ATT = T_LRU + 2 * COLS
T_MERGE = T_ATT + 2 * COLS
T_H = T_MERGE + COLS
T_HID = T_H + COLS

SCRATCH = 3 * HC * SEQ + (HC + 2) * 3 * P

ROWS = ["norm_mix_g", "norm_mlp_g", "conv_b", "lru_ba", "lru_bx", "lru_lambda", "conv0", "conv1", "conv2", "conv3"]
COL = {name: KT * n for n, name in enumerate(ROWS)}

SPLIT_CREDIT = CHUNKS
FREE = 1


class Chain:

    def __init__(self, eng, sem):
        self.eng, self.sem, self.n, self.offset = eng, sem, 0, 0

    def link(self, instruction):
        self.n += 1
        instruction.then_inc(self.sem, 1)
        self.eng.wait_ge(self.sem, self.n + self.offset)

    def enter(self, i, per):
        self.start, self.per, self.offset = self.n, per, i * per

    def leave(self, iterations):
        assert self.n - self.start == self.per, (self.n - self.start, self.per)
        self.n, self.offset = self.start + self.per * iterations, 0


def build(nc, x, norm_mix_g, w_in, conv_w, conv_b, lru_wa, lru_ba, lru_wx, lru_bx, lru_lambda,
          w_proj_attn, w_proj_lru, w_out, norm_mlp_g, w_up, w_down, norm_final_g, out):
    with ExitStack() as ctx:
        def sb(name, shape, dt=F32):
            return ctx.enter_context(nc.sbuf_tensor(name, shape, dt))

        def sem(name):
            return ctx.enter_context(nc.semaphore(name))

        raw = sb("raw", [P, CHUNKS, CK, NC])
        w_hi = sb("w_hi", [P, RING, CK, NC], F32R)
        w_lo = sb("w_lo", [P, RING, CK, NC], F32R)
        bufa_hi = sb("bufa_hi", [P, KT, SEQ], F32R)
        bufa_lo = sb("bufa_lo", [P, KT, SEQ], F32R)
        bufb_hi = sb("bufb_hi", [P, KT, SEQ], F32R)
        bufb_lo = sb("bufb_lo", [P, KT, SEQ], F32R)
        resid = sb("resid", [P, TB, D])
        merged = sb("merged", [P, TB, D])
        gate_a = sb("gate_a", [P, TB, D])
        block_n = sb("block_n", [P, TB, NC])
        scratch = sb("scratch", [P, SCRATCH])
        ident = sb("ident", [P, P])
        dist = sb("dist", [P, 3 * P])
        count = sb("count", [P, 3 * P])
        prm_rows = sb("prm_rows", [P, 2, P])
        prm = sb("prm", [P, len(ROWS) * KT])
        neg_ba = sb("neg_ba", [P, KT])
        half_bx = sb("half_bx", [P, KT])
        c_sp = sb("c_sp", [P, 2, KT])
        small = sb("small", [P, 5, KT])
        slopes = sb("slopes", [P, HEADS])
        sumsq = sb("sumsq", [P, 2, TB * COLS])
        rnorm = sb("rnorm", [P, 5, TB])
        rtmp = sb("rtmp", [P, 4, TB])
        negmax = sb("negmax", [P, HC, 2])
        denom = sb("denom", [P, HC, 2])
        rdenom = sb("rdenom", [P, HC, 2])

        tile = HC * SEQ
        ROW = SEQ + 8
        xr_pad = scratch[:, 0:HC * ROW].rearrange("p (b t) -> p b t", b=HC)

        def lru_tile(n):
            a = HC * ROW + n * tile
            return scratch[:, a:a + tile].rearrange("p (b t) -> p b t", b=HC)

        xc, rr, aa, ti = (lru_tile(n) for n in range(4))
        a_sq = scratch[:, 0:tile].rearrange("p (b t) -> p b t", b=HC)
        gate_w = gate_a[:, 0, :].rearrange("p (h b g j) -> p h b g j", h=2, b=HC, g=2)
        q_t = scratch[:, 0:tile].rearrange("p (h t) -> p h t", h=HC)
        k_t = scratch[:, tile:2 * tile].rearrange("p (h t) -> p h t", h=HC)
        v_n = scratch[:, 2 * tile:3 * tile].rearrange("p (b n) -> p b n", b=TB)
        pr = scratch[:, 3 * tile:3 * tile + HC * 3 * P].rearrange("p (h s) -> p h s", h=HC)
        pr_t = scratch[:, 3 * tile + HC * 3 * P:SCRATCH].rearrange("p (h s) -> p h s", h=2)
        dist_i = scratch[:, 0:3 * P].bitcast(I32)
        bits_i = scratch[:, 3 * P:6 * P].bitcast(I32)
        mask_a, mask_b, mask_c = (scratch[:, n * 3 * P:(n + 1) * 3 * P] for n in (2, 3, 4))

        acc = [[ctx.enter_context(nc.psum_tensor(f"acc{p}{t}", [P, NC], F32)) for t in range(TB)] for p in range(2)]
        aux = [ctx.enter_context(nc.psum_tensor(f"aux{n}", [P, NC], F32)) for n in range(4)]

        def head_bank(h):
            return aux[(2 + h) % 4]

        raw_landed = [sem(f"raw_landed{j}") for j in range(CHUNKS)]
        hi_ready, lo_ready, chunks_multiplied = sem("hi_ready"), sem("lo_ready"), sem("chunks_multiplied")
        acc_free = [[sem(f"acc_free{p}{t}") for t in range(TB)] for p in range(2)]
        x_landed = [sem(f"x_landed{c}") for c in range(COLS)]
        prm_landed, gf_landed, gate_w_landed, stored = sem("prm_landed"), sem("gf_landed"), sem("gate_w_landed"), sem("stored")
        id_zero, id_ready, iota_ready, slopes_ready = sem("id_zero"), sem("id_ready"), sem("iota_ready"), sem("slopes_ready")
        prm_turned, prm_ready, abs_ready, exp_l_ready, lru_prm_ready = (
            sem(n) for n in ("prm_turned", "prm_ready", "abs_ready", "exp_l_ready", "lru_prm_ready"))
        squares_ready, var_ready, root_ready, rnorm_ready = (
            sem(n) for n in ("squares_ready", "var_ready", "root_ready", "rnorm_ready"))
        block_ready, pe_turned, turned_act, turned_dve = (sem(n) for n in ("block_ready", "pe_turned", "turned_act", "turned_dve"))
        conv_begun, xc_ready, gates_done, gates_read, r_ready, a_ready = (
            sem(n) for n in ("conv_begun", "xc_ready", "gates_done", "gates_read", "r_ready", "a_ready"))
        a_sq_ready, m2_ready, root_gelu, lru_y, lru_y_hi, lru_y_lo = (
            sem(n) for n in ("a_sq_ready", "m2_ready", "root_gelu", "lru_y", "lru_y_hi", "lru_y_lo"))
        scores_done, max_ready, exp_done, p_ready, pt_done, pt_read, pv_done, y_hi, y_lo = (
            sem(n) for n in ("scores_done", "max_ready", "exp_done", "p_ready", "pt_done", "pt_read", "pv_done", "y_hi", "y_lo"))
        final_ready = sem("final_ready")
        dve_chain = sem("dve_chain")

        Q, K, V, XR, XG, GA, GL = (n * D for n in range(7))

        def value(unit, per_unit, add):
            base, i, per = unit
            return per_unit * base + add + i * (per_unit * per)

        def pair(unit):
            return unit[0] % 2

        def read_out(unit):
            base, i, per = unit
            assert per % 2 == 0
            return FREE + base // 2 + 1 + i * (per // 2)

        def mlp_groups(eng, group):
            group((U_MLP, 0, 0), T_HID, first=True)
            with eng.Fori(0, GROUPS - 2) as i:
                group((U_MLP + 2 * COLS, i, 2 * COLS), T_HID + COLS + i * COLS)
            group((U_MLP + 2 * COLS * (GROUPS - 1), 0, 0), T_HID + COLS * (GROUPS - 1), last=True)

        block = ctx.enter_context(nc.Block())

        @block.sync
        def _(sp):
            def load_unit(unit, w, row, col):
                for j in range(CHUNKS):
                    sp.wait_ge(lo_ready, value(unit, CHUNKS, j + 1))
                    src = w[ds(row + j * CK * P, CK * P), ds(col, NC)].rearrange("(k p) n -> p k n", p=P)
                    sp.dma_start(raw[:, j], src).then_inc(raw_landed[j], 16)

            xv = x[0].rearrange("(b p) n -> p b n", p=P)
            for c in range(COLS):
                sp.dma_start(resid[:, :, c * NC:(c + 1) * NC], xv[:, :, c * NC:(c + 1) * NC]).then_inc(x_landed[c], 16)
            with sp.Fori(0, COLS // 2) as i:
                for half in range(2):
                    for n, part in enumerate((XR, XG, GL)):
                        load_unit((U_LRU + 3 * half + n, i, 6), w_in[0], 0, part + half * NC + i * (2 * NC))
                        if half == 0 and n == 0:
                            sp.wait_ge(gates_done, FREE + i * (2 * HC))
                            for hh in range(2):
                                for g, w in enumerate((lru_wa, lru_wx)):
                                    src = w[0, ds(i * (2 * HC) + hh * HC, HC)].rearrange("b i j -> i b j")
                                    sp.dma_start(gate_w[:, hh, :, g, :], src).then_inc(gate_w_landed, 16)
            with sp.Fori(0, COLS // 2) as i:
                for n in range(2):
                    load_unit((U_PLRU + n, i, 2), w_proj_lru[0], 0, n * NC + i * (2 * NC))
            with sp.Fori(0, COLS) as i:
                for n, part in enumerate((Q, K, V, GA)):
                    load_unit((U_ATT + n, i, 4), w_in[0], 0, part + i * NC)
            for c in range(COLS):
                load_unit((U_PATT + c, 0, 0), w_proj_attn[0], 0, c * NC)
            for c in range(COLS):
                load_unit((U_OUT + c, 0, 0), w_out[0], 0, c * NC)
            sp.wait_ge(block_ready, COLS)
            sp.dma_start(merged[:, 0, :], norm_final_g.rearrange("(a n) -> a n", a=1).broadcast_to([P, D])).then_inc(gf_landed, 16)
            with sp.Fori(0, GROUPS) as i:
                for n in range(COLS):
                    load_unit((U_MLP + n, i, 2 * COLS), w_up[0], 0, n * NC + i * D)
                for n in range(COLS):
                    load_unit((U_MLP + COLS + n, i, 2 * COLS), w_down[0], i * D, n * NC)
            ov = out[0].rearrange("(b p) n -> p b n", p=P)
            for c in range(COLS):
                sp.wait_ge(final_ready, c + 1)
                sp.dma_start(ov[:, :, c * NC:(c + 1) * NC], resid[:, :, c * NC:(c + 1) * NC]).then_inc(stored, 16)
            sp.wait_ge(stored, 16 * COLS)

        @block.gpsimd
        def _(pool):
            for buffer_free in (gates_done, gates_read, lru_y_lo, scores_done, pv_done, m2_ready, pt_done, y_lo,
                                *acc_free[0], *acc_free[1]):
                pool.sem_inc(buffer_free, FREE)
            nc.gpsimd.memset(ident[:, :], 0.0).then_inc(id_zero, 1)
            pool.wait_ge(id_zero, 1)
            nc.gpsimd.affine_select(out=ident[:, :], in_=ident[:, :], compare_op=ALU.not_equal, fill=1.0,
                                    base=0, pattern=[[-1, P]], channel_multiplier=1).then_inc(id_ready, 1)
            for n, base in enumerate((0, P, 0)):
                nc.gpsimd.iota(dist_i[:, n * P:(n + 1) * P], pattern=[[-1, P]], base=base,
                               channel_multiplier=1).then_inc(iota_ready, 1)
            for h in range(HEADS):
                last = nc.gpsimd.memset(slopes[:, h:h + 1], 2.0 ** (-8.0 * (h + 1) / HEADS))
            last.then_inc(slopes_ready, 1)
            with pool.Fori(0, COLS) as c:
                pool.wait_ge(a_ready, c + 1)
                nc.gpsimd.tensor_tensor(a_sq, aa, aa, ALU.mult).then_inc(a_sq_ready, 1)

        @block.tensor
        def _(pe):
            def chunks(unit, first, last, hi, lo):
                for j in range(first, last):
                    pe.wait_ge(lo_ready, value(unit, CHUNKS, j + 1 + SPLIT_CREDIT))
                    for b in range(TB):
                        if j == 0:
                            pe.wait_ge(acc_free[pair(unit)][b], read_out(unit) - 1)
                        for kk in range(CK):
                            k = j * CK + kk
                            a_hi, a_lo = hi[:, k, b * P:(b + 1) * P], lo[:, k, b * P:(b + 1) * P]
                            b_hi, b_lo = w_hi[:, j % RING, kk, :], w_lo[:, j % RING, kk, :]
                            dst = acc[pair(unit)][b][:, :]
                            nc.tensor.matmul(dst, a_hi, b_hi, start=k == 0, stop=False)
                            nc.tensor.matmul(dst, a_hi, b_lo, start=False, stop=False)
                            mm = nc.tensor.matmul(dst, a_lo, b_hi, start=False, stop=k == KT - 1)
                    mm.then_inc(chunks_multiplied, 1)

            def turn(number, src, dve_reads):
                for b in range(2):
                    if dve_reads is not None:
                        pe.wait_ge(turned_act, number * 2 + b - 1)
                        pe.wait_ge(turned_dve, dve_reads + b - 1)
                    for k in range(2):
                        for t in range(TB):
                            tr = nc.tensor.transpose(aux[b][:, k * SEQ + t * P:k * SEQ + (t + 1) * P],
                                                     src[:, t, (2 * b + k) * P:(2 * b + k + 1) * P], ident[:, :])
                    tr.then_inc(pe_turned, 1)

            def block_turn(number, unit, dve_reads):
                for b in range(TB):
                    pe.wait_ge(acc_free[pair(unit)][b], read_out(unit))
                turn(number, block_n, dve_reads)

            A, B = (bufa_hi, bufa_lo), (bufb_hi, bufb_lo)

            pe.wait_ge(id_ready, 1)
            pe.wait_ge(prm_landed, 16 * len(ROWS))
            nc.tensor.transpose(aux[2][:, 0:P], prm_rows[:, 0, :], ident[:, :])
            rest = len(ROWS) * KT - P
            nc.tensor.transpose(aux[2][:, P:P + rest], prm_rows[0:rest, 1, :], ident[0:rest, 0:rest]).then_inc(prm_turned, 1)
            for c in range(COLS):
                pe.wait_ge(x_landed[c], 16)
                turn(T_X + c, resid[:, :, c * NC:(c + 1) * NC], 2 * c if c else None)
            pe.wait_ge(turned_dve, 2 * COLS)

            with pe.Fori(0, COLS // 2) as i:
                for half in range(2):
                    xr, xg, gl = ((U_LRU + 3 * half + n, i, 6) for n in range(3))
                    turn_xr = T_LRU + 2 * half + i * 4
                    blk = half * HC + i * (2 * HC)
                    dve_reads = 2 * T_LRU + 2 * half + i * 4
                    chunks(xr, 0, 8, *A)
                    chunks(xg, 0, 2, *A)
                    block_turn(turn_xr, xr, dve_reads)
                    chunks(xg, 2, 6, *A)
                    if half == 0:
                        pe.wait_ge(gate_w_landed, 64 + i * 64)
                    for b in range(HC):
                        pe.wait_ge(xc_ready, blk + b + 1)
                        pe.wait_ge(gates_read, FREE + blk + max(b - 1, 0))
                        for g in range(2):
                            mm = nc.tensor.matmul(aux[2 + b % 2][:, g * SEQ:(g + 1) * SEQ], gate_w[:, half, b, g, :],
                                                  xc[:, b, :], start=True, stop=True)
                        mm.then_inc(gates_done, 1)
                        if b % 2:
                            chunks(xg, 6 + b // 2, 7 + b // 2, *A)
                    chunks(gl, 0, 2, *A)
                    block_turn(turn_xr + 1, xg, dve_reads + 2)
                    chunks(gl, 2, 8, *A)

            pe.wait_ge(lru_y_lo, FREE + COLS)
            with pe.Fori(0, COLS // 2) as i:
                for n in range(2):
                    chunks((U_PLRU + n, i, 2), 0, 8, *B)

            with pe.Fori(0, COLS) as i:
                q, k, v, ga = ((U_ATT + n, i, 4) for n in range(4))
                turn_q = T_ATT + i * 2
                dve_reads = 2 * T_LRU + 2 * COLS + i * 4
                head = i * HC
                chunks(q, 0, 8, *A)
                chunks(k, 0, 2, *A)
                pe.wait_ge(y_lo, FREE + head)
                block_turn(turn_q, q, dve_reads)
                chunks(k, 2, 8, *A)
                chunks(v, 0, 2, *A)
                block_turn(turn_q + 1, k, dve_reads + 2)
                chunks(v, 2, 4, *A)
                pe.wait_ge(turned_act, turn_q * 2 + 4)
                pe.wait_ge(turned_dve, dve_reads + 4)
                for h in range(HC):
                    nc.tensor.matmul(head_bank(h)[:, 0:P], q_t[:, h, 0:P], k_t[:, h, 0:P], start=True, stop=True)
                    nc.tensor.matmul(head_bank(h)[:, P:3 * P], q_t[:, h, P:SEQ], k_t[:, h, :], start=True,
                                     stop=True).then_inc(scores_done, 1)
                    if h == 1:
                        chunks(v, 4, 5, *A)
                chunks(v, 5, 8, *A)

                def turn_probs(h):
                    pe.wait_ge(p_ready, head + h + 1)
                    for n in range(3):
                        tr = nc.tensor.transpose(head_bank(h)[:, n * P:(n + 1) * P], pr[:, h, n * P:(n + 1) * P], ident[:, :])
                    tr.then_inc(pt_done, 1)

                def times_values(h):
                    pe.wait_ge(pt_read, head + h + 1)
                    for b in range(TB):
                        pe.wait_ge(acc_free[pair(v)][b], read_out(v))
                    dst = head_bank(h)
                    nc.tensor.matmul(dst[:, 0:SEQ], v_n[:, 0, h * P:(h + 1) * P], pr_t[:, h % 2, 0:2 * P], start=True,
                                     stop=False, skip_group_check=True)
                    nc.tensor.matmul(dst[:, P:SEQ], v_n[:, 1, h * P:(h + 1) * P], pr_t[:, h % 2, 2 * P:3 * P], start=False,
                                     stop=True, skip_group_check=True).then_inc(pv_done, 1)

                chunks(ga, 0, 2, *A)
                turn_probs(0)
                chunks(ga, 2, 3, *A)
                turn_probs(1)
                chunks(ga, 3, 4, *A)
                times_values(0)
                turn_probs(2)
                chunks(ga, 4, 5, *A)
                times_values(1)
                turn_probs(3)
                chunks(ga, 5, 6, *A)
                times_values(2)
                chunks(ga, 6, 7, *A)
                times_values(3)
                chunks(ga, 7, 8, *A)

            dve0 = 2 * T_LRU + 2 * COLS - 2 * T_ATT
            pe.wait_ge(y_lo, FREE + HEADS)
            for c in range(COLS):
                unit = (U_PATT + c, 0, 0)
                chunks(unit, 0, 2, *B)
                if c:
                    pe.wait_ge(block_ready, c)
                    turn(T_MERGE + c - 1, block_n, 2 * (T_MERGE + c - 1) + dve0)
                chunks(unit, 2, 8, *B)

            for c in range(COLS):
                unit = (U_OUT + c, 0, 0)
                if c == 0:
                    pe.wait_ge(turned_dve, 2 * (T_H - 1) + dve0)
                chunks(unit, 0, 2, *A)
                if c == 0:
                    pe.wait_ge(block_ready, COLS)
                    turn(T_H - 1, block_n, 2 * (T_H - 1) + dve0)
                else:
                    before = (U_OUT + c - 1, 0, 0)
                    for b in range(TB):
                        pe.wait_ge(acc_free[pair(before)][b], read_out(before))
                    turn(T_H + c - 1, resid[:, :, (c - 1) * NC:c * NC], 2 * (T_H + c - 1) + dve0)
                chunks(unit, 2, 6, *A)
                if c == 0:
                    pe.wait_ge(turned_dve, 2 * T_H + dve0)
                chunks(unit, 6, 8, *A)

            def group(unit0, turn0, first=False, last=False):
                base, i, per = unit0
                for n in range(COLS):
                    unit = (base + n, i, per)
                    if first and n == 0:
                        pe.wait_ge(turned_dve, 2 * (T_HID - 1) + dve0)
                    chunks(unit, 0, 2, *B)
                    if n:
                        pe.wait_ge(block_ready, turn0 + (n - T_HID + COLS))
                        turn(turn0 + (n - 1), block_n, turn0 * 2 + (2 * (n - 1) + dve0))
                    elif first:
                        before = (U_MLP - 1, 0, 0)
                        for b in range(TB):
                            pe.wait_ge(acc_free[pair(before)][b], read_out(before))
                        turn(T_HID - 1, resid[:, :, D - NC:D], 2 * (T_HID - 1) + dve0)
                    chunks(unit, 2, 6, *B)
                    if first and n == 0:
                        pe.wait_ge(turned_dve, 2 * T_HID + dve0)
                    chunks(unit, 6, 8, *B)
                for n in range(COLS):
                    unit = (base + COLS + n, i, per)
                    if n == 0:
                        pe.wait_ge(turned_dve, turn0 * 2 + (2 * (COLS - 1) + dve0))
                    chunks(unit, 0, 2, *A)
                    if n == 0:
                        pe.wait_ge(block_ready, turn0 + (2 * COLS - T_HID))
                        turn(turn0 + (COLS - 1), block_n, turn0 * 2 + (2 * (COLS - 1) + dve0))
                    chunks(unit, 2, 6, *A)
                    if n == 0:
                        pe.wait_ge(turned_dve, turn0 * 2 + (2 * COLS + dve0))
                    chunks(unit, 6, 8, *A)

            mlp_groups(pe, group)

        @block.scalar
        def _(act):
            def cast(unit, first, last):
                for ch in range(first, last):
                    j = ch % CHUNKS
                    act.wait_ge(raw_landed[j], value(unit, 16, 16 * (ch // CHUNKS + 1)))
                    if ch >= RING:
                        act.wait_ge(chunks_multiplied, value(unit, CHUNKS, ch - RING + 1))
                    nc.scalar.activation(w_hi[:, j % RING], raw[:, j], ACT.Copy).then_inc(hi_ready, 1)

            def acc_done(unit):
                act.wait_ge(chunks_multiplied, value(unit, CHUNKS, CHUNKS))

            def block_out(unit, turn, factor):
                acc_done(unit)
                act.wait_ge(pe_turned, turn * 2)
                nc.scalar.activation(block_n[:, 0, :], acc[pair(unit)][0][:, :], ACT.Copy,
                                     scale=rnorm[:, factor, 0:1]).then_inc(acc_free[pair(unit)][0], 1)

            def turn_hi(turn, dst, tile0, scale=1.0, gain=None):
                for b in range(2):
                    act.wait_ge(pe_turned, turn * 2 + b + 1)
                    if gain is None:
                        n = tile0 + 2 * b
                        nc.scalar.activation(dst[:, n:n + 2, :], aux[b][:, :].rearrange("p (k t) -> p k t", k=2),
                                             ACT.Copy, scale=scale).then_inc(turned_act, 1)
                    else:
                        for k in range(2):
                            n = tile0 + 2 * b + k
                            last = nc.scalar.activation(dst[:, n, :], aux[b][:, k * SEQ:(k + 1) * SEQ], ACT.Copy,
                                                        scale=prm[:, gain + n:gain + n + 1])
                        last.then_inc(turned_act, 1)

            def turn_copy(turn, dst):
                act.wait_ge(pe_turned, turn * 2 + 1)
                nc.scalar.activation(dst[:, 0:2], aux[0][:, :].rearrange("p (k t) -> p k t", k=2), ACT.Copy).then_inc(turned_act, 2)

            def root(n):
                act.wait_ge(var_ready, n)
                nc.scalar.activation(rtmp[:, 1, :], rtmp[:, 0, :], ACT.Sqrt).then_inc(root_ready, 1)

            singles = [norm_mix_g, norm_mlp_g, conv_b, lru_ba, lru_bx, lru_lambda]
            for n in range(len(ROWS)):
                src = singles[n][0] if n < len(singles) else conv_w[0, n - len(singles)]
                r = n * KT % P
                act.dma_start(prm_rows[r:r + KT, n * KT // P, :], src.rearrange("(k p) -> k p", p=P)).then_inc(prm_landed, 16)
            act.wait_ge(prm_ready, 1)
            nc.scalar.activation(small[:, 0, :], prm[:, COL["lru_lambda"]:COL["lru_lambda"] + KT], ACT.Abs).then_inc(abs_ready, 1)
            act.wait_ge(abs_ready, 1)
            nc.scalar.activation(small[:, 1, :], small[:, 0, :], ACT.Exp, scale=-1.0).then_inc(exp_l_ready, 1)
            for c in range(COLS):
                turn_hi(T_X + c, bufa_hi, HC * c, gain=COL["norm_mix_g"])
            cast((0, 0, 0), 0, RING)
            for c in range(COLS):
                act.wait_ge(x_landed[c], 16)
            for b in range(TB):
                nc.scalar.activation(merged[:, b, :], resid[:, b, :], ACT.Square,
                                     accum_out=sumsq[:, 0, b:b + 1]).then_inc(squares_ready, 1)
            root(1)

            act.wait_ge(rnorm_ready, 1)
            act.wait_ge(lru_prm_ready, 1)
            with act.Fori(0, COLS // 2) as i:
                for half in range(2):
                    xr, xg, gl = ((U_LRU + 3 * half + n, i, 6) for n in range(3))
                    turn = T_LRU + 2 * half + i * 4
                    blk = half * HC + i * (2 * HC)
                    col = half + i * 2
                    cast(xr, 4, 12)
                    block_out(xr, turn, 0)
                    cast(xg, 4, 6)
                    act.wait_ge(lru_y_lo, FREE + col)
                    turn_copy(turn, xr_pad[:, :, 8:ROW])
                    act.wait_ge(turned_act, turn * 2 + 2)
                    act.wait_ge(turned_dve, 2 * T_LRU + 2 + 2 * half + i * 4)
                    for b in range(HC):
                        last = nc.scalar.activation(xc[:, b, :], xr_pad[:, b, 8:ROW], ACT.Identity,
                                                    scale=prm[:, ds(COL["conv3"] + b + blk, 1)],
                                                    bias=prm[:, ds(COL["conv_b"] + b + blk, 1)])
                    last.then_inc(conv_begun, 1)
                    cast(xg, 6, 10)
                    for b in range(HC):
                        act.wait_ge(gates_done, FREE + blk + b + 1)
                        nc.scalar.activation(rr[:, b, :], aux[2 + b % 2][:, 0:SEQ], ACT.Exp, scale=-1.0,
                                             bias=neg_ba[:, ds(blk + b, 1)])
                        nc.scalar.activation(ti[:, b, :], aux[2 + b % 2][:, SEQ:2 * SEQ], ACT.Tanh, scale=0.5,
                                             bias=half_bx[:, ds(blk + b, 1)]).then_inc(gates_read, 1)
                        if b % 2:
                            cast(xg, 10 + b // 2, 11 + b // 2)
                    block_out(xg, turn + 1, 0)
                    cast(gl, 4, 6)
                    for b in range(HC):
                        act.wait_ge(r_ready, blk + b + 1)
                        nc.scalar.activation(aa[:, b, :], rr[:, b, :], ACT.Exp, scale=c_sp[:, 0, ds(blk + b, 1)])
                        last = nc.scalar.activation(rr[:, b, :], rr[:, b, :], ACT.Tanh, scale=c_sp[:, 1, ds(blk + b, 1)])
                    last.then_inc(a_ready, 1)
                    cast(gl, 6, 8)
                    act.wait_ge(m2_ready, FREE + col + 1)
                    nc.scalar.activation(rr, rr, ACT.Sqrt).then_inc(root_gelu, 1)
                    for b in range(2):
                        act.wait_ge(pe_turned, turn * 2 + 3 + b)
                        nc.scalar.activation(xc[:, 2 * b:2 * b + 2, :], aux[b][:, :].rearrange("p (k t) -> p k t", k=2),
                                             ACT.Gelu_apprx_tanh).then_inc(turned_act, 1)
                    cast(gl, 8, 11)
                    act.wait_ge(lru_y, col + 1)
                    nc.scalar.activation(bufb_hi[:, ds(blk, HC), :], ti, ACT.Copy).then_inc(lru_y_hi, 1)
                    cast(gl, 11, 12)
                    acc_done(gl)
                    for b in range(TB):
                        nc.scalar.activation(merged[:, b, ds(half * NC + i * (2 * NC), NC)], acc[pair(gl)][b][:, :], ACT.Tanh,
                                             scale=rnorm[:, 2, b:b + 1]).then_inc(acc_free[pair(gl)][b], 1)

            with act.Fori(0, COLS // 2) as i:
                for n in range(2):
                    cast((U_PLRU + n, i, 2), 4, 12)

            act.wait_ge(lru_y_lo, FREE + COLS)
            with act.Fori(0, COLS) as i:
                q, k, v, ga = ((U_ATT + n, i, 4) for n in range(4))
                turn = T_ATT + i * 2
                head = i * HC

                def exps(h):
                    act.wait_ge(max_ready, head + h + 1)
                    nc.scalar.activation(pr[:, h, 0:P], pr[:, h, 0:P], ACT.Exp, bias=negmax[:, h, 0:1])
                    nc.scalar.activation(pr[:, h, P:3 * P], pr[:, h, P:3 * P], ACT.Exp,
                                         bias=negmax[:, h, 1:2]).then_inc(exp_done, 1)

                def probs_out(h):
                    act.wait_ge(pt_done, FREE + head + h + 1)
                    act.wait_ge(pv_done, FREE + head + max(h - 1, 0))
                    nc.scalar.activation(pr_t[:, h % 2, :], head_bank(h)[:, 0:3 * P], ACT.Copy).then_inc(pt_read, 1)

                def y_out(h):
                    act.wait_ge(pv_done, FREE + head + h + 1)
                    nc.scalar.activation(bufb_hi[:, ds(head + h, 1), :], head_bank(h)[:, 0:SEQ].rearrange("p (k t) -> p k t", k=1),
                                         ACT.Copy).then_inc(y_hi, 1)

                cast(q, 4, 12)
                block_out(q, turn, 1)
                cast(k, 4, 6)
                act.wait_ge(scores_done, FREE + head)
                turn_copy(turn, q_t)
                cast(k, 6, 12)
                block_out(k, turn + 1, 0)
                cast(v, 4, 6)
                turn_copy(turn + 1, k_t)
                cast(v, 6, 10)
                exps(0)
                cast(v, 10, 11)
                exps(1)
                cast(v, 11, 12)
                acc_done(v)
                act.wait_ge(pv_done, FREE + head)
                nc.scalar.activation(v_n[:, 0, :], acc[pair(v)][0][:, :], ACT.Copy,
                                     scale=rnorm[:, 0, 0:1]).then_inc(acc_free[pair(v)][0], 1)
                exps(2)
                cast(ga, 4, 5)
                exps(3)
                cast(ga, 5, 6)
                probs_out(0)
                cast(ga, 6, 7)
                probs_out(1)
                cast(ga, 7, 8)
                y_out(0)
                probs_out(2)
                cast(ga, 8, 9)
                y_out(1)
                probs_out(3)
                cast(ga, 9, 10)
                y_out(2)
                cast(ga, 10, 11)
                y_out(3)
                cast(ga, 11, 12)
                acc_done(ga)
                for b in range(TB):
                    nc.scalar.activation(gate_a[:, b, ds(i * NC, NC)], acc[pair(ga)][b][:, :], ACT.Tanh,
                                         scale=rnorm[:, 2, b:b + 1]).then_inc(acc_free[pair(ga)][b], 1)

            for c in range(COLS):
                unit = (U_PATT + c, 0, 0)
                cast(unit, 4, 6)
                if c:
                    turn_hi(T_MERGE + c - 1, bufa_hi, HC * (c - 1), scale=0.5)
                cast(unit, 6, 12)

            for c in range(COLS):
                unit = (U_OUT + c, 0, 0)
                cast(unit, 4, 6)
                if c == 0:
                    turn_hi(T_H - 1, bufa_hi, HC * (COLS - 1), scale=0.5)
                else:
                    turn_hi(T_H + c - 1, bufb_hi, HC * (c - 1), gain=COL["norm_mlp_g"])
                cast(unit, 6, 12)
                for b in range(TB):
                    act.wait_ge(acc_free[pair(unit)][b], read_out(unit))
                    nc.scalar.activation(block_n[:, b, :], resid[:, b, c * NC:(c + 1) * NC], ACT.Square,
                                         accum_out=sumsq[:, 1, b * COLS + c:b * COLS + c + 1]).then_inc(squares_ready, 1)

            def group(unit0, turn0, first=False, last=False):
                base, i, per = unit0
                for n in range(COLS):
                    unit = (base + n, i, per)
                    cast(unit, 4, 6)
                    if n:
                        turn_hi(turn0 + (n - 1), bufa_hi, HC * (n - 1))
                    elif first:
                        turn_hi(T_HID - 1, bufb_hi, HC * (COLS - 1), gain=COL["norm_mlp_g"])
                        cast(unit, 6, 7)
                        root(2)
                    cast(unit, 7 if first and n == 0 else 6, 12)
                    acc_done(unit)
                    if first and n == 0:
                        act.wait_ge(rnorm_ready, 2)
                    act.wait_ge(pe_turned, turn0 * 2 + 2 * n)
                    for b in range(TB):
                        nc.scalar.activation(block_n[:, b, :], acc[pair(unit)][b][:, :], ACT.Relu,
                                             scale=rnorm[:, 3, b:b + 1]).then_inc(acc_free[pair(unit)][b], 1)
                for n in range(COLS):
                    unit = (base + COLS + n, i, per)
                    cast(unit, 4, 6)
                    if n == 0:
                        turn_hi(turn0 + (COLS - 1), bufa_hi, HC * (COLS - 1))
                    cast(unit, 6, 8 if last and n == COLS - 1 else 12)
                    if last:
                        for b in range(TB):
                            act.wait_ge(acc_free[pair(unit)][b], read_out(unit))
                            nc.scalar.activation(block_n[:, b, :], resid[:, b, n * NC:(n + 1) * NC], ACT.Square,
                                                 accum_out=sumsq[:, 0, b * COLS + n:b * COLS + n + 1]).then_inc(squares_ready, 1)

            mlp_groups(act, group)
            root(3)

        @block.vector
        def _(dve):
            chain = Chain(dve, dve_chain)
            link = chain.link

            def split(unit, first, last):
                for ch in range(first, last):
                    j = ch % CHUNKS
                    dve.wait_ge(hi_ready, value(unit, CHUNKS, ch + 1))
                    nc.vector.tensor_tensor(w_lo[:, j % RING], raw[:, j], w_hi[:, j % RING].bitcast(F32),
                                            ALU.subtract).then_inc(lo_ready, 1)

            def acc_done(unit):
                dve.wait_ge(chunks_multiplied, value(unit, CHUNKS, CHUNKS))

            def block_out(unit, turn, factor):
                acc_done(unit)
                dve.wait_ge(pe_turned, turn * 2)
                nc.vector.tensor_scalar(block_n[:, 1, :], acc[pair(unit)][1][:, :], rnorm[:, factor, 1:2], None,
                                        ALU.mult).then_inc(acc_free[pair(unit)][1], 1)

            def turn_lo(turn, dst_lo, dst_hi, tile0, scale=1.0, gain=None):
                for b in range(2):
                    dve.wait_ge(turned_act, turn * 2 + b + 1)
                    if gain is None:
                        n = tile0 + 2 * b
                        nc.vector.scalar_tensor_tensor(
                            out=dst_lo[:, n:n + 2, :], in0=aux[b][:, :].rearrange("p (k t) -> p k t", k=2), scalar=scale,
                            in1=dst_hi[:, n:n + 2, :].bitcast(F32), op0=ALU.mult, op1=ALU.subtract).then_inc(turned_dve, 1)
                    else:
                        for k in range(2):
                            n = tile0 + 2 * b + k
                            last = nc.vector.scalar_tensor_tensor(
                                out=dst_lo[:, n, :], in0=aux[b][:, k * SEQ:(k + 1) * SEQ], scalar=prm[:, gain + n:gain + n + 1],
                                in1=dst_hi[:, n, :].bitcast(F32), op0=ALU.mult, op1=ALU.subtract)
                        last.then_inc(turned_dve, 1)

            def turn_copy(turn, dst):
                dve.wait_ge(pe_turned, turn * 2 + 2)
                nc.vector.tensor_copy(dst[:, 2:4], aux[1][:, :].rearrange("p (k t) -> p k t", k=2)).then_inc(turned_dve, 2)

            def variance(squares, total):
                dve.wait_ge(squares_ready, squares)
                link(nc.vector.tensor_reduce(rtmp[:, 0, :], total, AX_X, ALU.add))
                nc.vector.tensor_scalar(rtmp[:, 0, :], rtmp[:, 0, :], 1.0 / D, EPS, ALU.mult, ALU.add).then_inc(var_ready, 1)

            def rsqrt(n, dst):
                dve.wait_ge(root_ready, n)
                link(nc.vector.reciprocal(rtmp[:, 2, :], rtmp[:, 1, :]))
                link(nc.vector.tensor_tensor(rtmp[:, 2, :], rtmp[:, 0, :], rtmp[:, 2, :], ALU.mult))
                link(nc.vector.tensor_tensor(rtmp[:, 2, :], rtmp[:, 1, :], rtmp[:, 2, :], ALU.add))
                link(nc.vector.tensor_scalar(rtmp[:, 2, :], rtmp[:, 2, :], 0.5, None, ALU.mult))
                return nc.vector.reciprocal(dst, rtmp[:, 2, :])

            nc.vector.memset(rtmp[:, 3, :], 0.0).then_inc(lo_ready, SPLIT_CREDIT)

            dve.wait_ge(prm_turned, 1)
            nc.vector.tensor_copy(prm[:, :], aux[2][:, 0:len(ROWS) * KT]).then_inc(prm_ready, 1)
            dve.wait_ge(prm_ready, 1)
            for c in range(COLS):
                turn_lo(T_X + c, bufa_lo, bufa_hi, HC * c, gain=COL["norm_mix_g"])
            split((0, 0, 0), 0, RING)
            variance(TB, sumsq[:, 0, 0:TB].rearrange("p (b c) -> p b c", c=1))

            dve.wait_ge(iota_ready, 3)
            link(nc.vector.tensor_scalar(bits_i, dist_i, 3, None, ALU.bitwise_and))
            link(nc.vector.tensor_scalar(mask_a, bits_i, 0.0, None, ALU.is_equal))
            link(nc.vector.tensor_scalar(bits_i, dist_i, 15, None, ALU.bitwise_and))
            link(nc.vector.tensor_scalar(mask_b, bits_i, 0.0, None, ALU.is_equal))
            link(nc.vector.tensor_tensor(mask_a, mask_a, mask_b, ALU.add))
            link(nc.vector.tensor_copy(mask_c, dist_i))
            link(nc.vector.tensor_scalar(mask_b, mask_c, float(P), None, ALU.is_le))
            link(nc.vector.tensor_tensor(mask_a, mask_a, mask_b, ALU.add))
            link(nc.vector.tensor_scalar(mask_b, mask_c, 0.0, None, ALU.is_ge))
            link(nc.vector.tensor_tensor(count[:, :], mask_a, mask_b, ALU.mult))
            link(nc.vector.tensor_scalar(mask_b, count[:, :], 0.0, MASKED, ALU.is_equal, ALU.mult))
            link(nc.vector.tensor_tensor(dist[:, :], mask_b, mask_c, ALU.subtract))

            e, s, s2, p = (small[:, n, :] for n in (1, 2, 3, 4))
            dve.wait_ge(exp_l_ready, 1)
            link(nc.vector.tensor_scalar(s2, e, 2.0, None, ALU.add))
            link(nc.vector.reciprocal(s, s2))
            link(nc.vector.tensor_tensor(s, s, e, ALU.mult))
            link(nc.vector.tensor_tensor(s2, s, s, ALU.mult))
            link(nc.vector.tensor_scalar(p, s2, 1.0 / 15, None, ALU.mult))
            for odd in (13, 11, 9, 7, 5, 3):
                link(nc.vector.scalar_tensor_tensor(out=p, in0=p, scalar=1.0 / odd, in1=s2, op0=ALU.add, op1=ALU.mult))
            link(nc.vector.scalar_tensor_tensor(out=p, in0=p, scalar=1.0, in1=s, op0=ALU.add, op1=ALU.mult))
            lam = prm[:, COL["lru_lambda"]:COL["lru_lambda"] + KT]
            link(nc.vector.tensor_scalar(s, lam, -1.0, 0.0, ALU.mult, ALU.max))
            link(nc.vector.scalar_tensor_tensor(out=p, in0=p, scalar=2.0, in1=s, op0=ALU.mult, op1=ALU.add))
            nc.vector.tensor_scalar(c_sp[:, 0, :], p, -LRU_C, None, ALU.mult)
            nc.vector.tensor_scalar(c_sp[:, 1, :], p, LRU_C, None, ALU.mult)
            nc.vector.tensor_scalar(neg_ba[:, :], prm[:, COL["lru_ba"]:COL["lru_ba"] + KT], -1.0, None, ALU.mult)
            nc.vector.tensor_scalar(half_bx[:, :], prm[:, COL["lru_bx"]:COL["lru_bx"] + KT], 0.5, None,
                                    ALU.mult).then_inc(lru_prm_ready, 1)
            link(rsqrt(1, rnorm[:, 0, :]))
            nc.vector.tensor_scalar(rnorm[:, 1, :], rnorm[:, 0, :], QK_SCALE, None, ALU.mult)
            nc.vector.tensor_scalar(rnorm[:, 2, :], rnorm[:, 0, :], 0.5, None, ALU.mult).then_inc(rnorm_ready, 1)

            with dve.Fori(0, COLS // 2) as i:
                chain.enter(i, 2 * 10)
                for half in range(2):
                    xr, xg, gl = ((U_LRU + 3 * half + n, i, 6) for n in range(3))
                    turn = T_LRU + 2 * half + i * 4
                    blk = half * HC + i * (2 * HC)
                    col = half + i * 2
                    split(xr, 4, 12)
                    block_out(xr, turn, 0)
                    dve.wait_ge(m2_ready, FREE + col)
                    link(nc.vector.memset(xr_pad[:, :, 8 - PAD:8], 0.0))
                    split(xg, 4, 6)
                    turn_copy(turn, xr_pad[:, :, 8:ROW])
                    split(xg, 6, 7)
                    dve.wait_ge(conv_begun, col + 1)
                    for lag in range(1, CONV_W):
                        for b in range(HC):
                            tap = nc.vector.scalar_tensor_tensor(
                                out=xc[:, b, :], in0=xr_pad[:, b, 8 - lag:ROW - lag],
                                scalar=prm[:, ds(COL[f"conv{PAD - lag}"] + b + blk, 1)], in1=xc[:, b, :],
                                op0=ALU.mult, op1=ALU.add)
                            if lag == PAD:
                                tap.then_inc(xc_ready, 1)
                        if lag != PAD:
                            link(tap)
                            split(xg, 6 + lag, 7 + lag)
                    split(xg, 9, 10)
                    for b in range(HC):
                        dve.wait_ge(gates_read, FREE + blk + b + 1)
                        link(nc.vector.tensor_scalar(rr[:, b, :], rr[:, b, :], 1.0, None, ALU.add))
                        nc.vector.reciprocal(rr[:, b, :], rr[:, b, :]).then_inc(r_ready, 1)
                        if b % 2:
                            split(xg, 10 + b // 2, 11 + b // 2)
                    block_out(xg, turn + 1, 0)
                    split(gl, 4, 6)
                    link(nc.vector.scalar_tensor_tensor(out=ti, in0=ti, scalar=1.0, in1=xc, op0=ALU.add, op1=ALU.mult))
                    dve.wait_ge(a_sq_ready, col + 1)
                    nc.vector.scalar_tensor_tensor(out=rr, in0=a_sq, scalar=1.0, in1=rr, op0=ALU.add,
                                                   op1=ALU.mult).then_inc(m2_ready, 1)
                    split(gl, 6, 9)
                    dve.wait_ge(root_gelu, col + 1)
                    link(nc.vector.scalar_tensor_tensor(out=ti, in0=ti, scalar=0.5, in1=rr, op0=ALU.mult, op1=ALU.mult))
                    for b in range(HC):
                        last = nc.vector.tensor_tensor_scan(rr[:, b, :], aa[:, b, :], ti[:, b, :], 0.0, ALU.mult, ALU.add)
                    link(last)
                    dve.wait_ge(turned_act, turn * 2 + 4)
                    nc.vector.tensor_tensor(ti, rr, xc, ALU.mult).then_inc(lru_y, 1)
                    split(gl, 9, 11)
                    dve.wait_ge(lru_y_hi, col + 1)
                    nc.vector.tensor_tensor(bufb_lo[:, ds(blk, HC), :], ti, bufb_hi[:, ds(blk, HC), :].bitcast(F32),
                                            ALU.subtract).then_inc(lru_y_lo, 1)
                    split(gl, 11, 12)
                chain.leave(COLS // 2)

            for b in range(TB):
                dve.wait_ge(acc_free[1][b], FREE + U_PLRU // 2)
            with dve.Fori(0, COLS // 2) as i:
                for n in range(2):
                    unit = (U_PLRU + n, i, 2)
                    split(unit, 4, 12)
                    acc_done(unit)
                    for b in range(TB):
                        part = merged[:, b, ds(n * NC + i * (2 * NC), NC)]
                        nc.vector.scalar_tensor_tensor(out=part, in0=part, scalar=1.0, in1=acc[pair(unit)][b][:, :],
                                                       op0=ALU.add, op1=ALU.mult).then_inc(acc_free[pair(unit)][b], 1)

            dve.wait_ge(slopes_ready, 1)
            with dve.Fori(0, COLS) as i:
                chain.enter(i, HC * 4)
                q, k, v, ga = ((U_ATT + n, i, 4) for n in range(4))
                turn = T_ATT + i * 2
                head = i * HC

                def bias_and_max(h):
                    dve.wait_ge(scores_done, FREE + head + h + 1)
                    dve.wait_ge(pt_done, FREE + head)
                    link(nc.vector.scalar_tensor_tensor(out=pr[:, h, :], in0=dist[:, :], scalar=slopes[:, ds(head + h, 1)],
                                                        in1=head_bank(h)[:, 0:3 * P], op0=ALU.mult, op1=ALU.add))
                    nc.vector.tensor_reduce(negmax[:, h, 0:1], pr[:, h, 0:P], AX_X, ALU.max)
                    link(nc.vector.tensor_reduce(negmax[:, h, 1:2], pr[:, h, P:3 * P], AX_X, ALU.max))
                    nc.vector.tensor_scalar(negmax[:, h, :], negmax[:, h, :], -1.0, None, ALU.mult).then_inc(max_ready, 1)

                def normalise(h):
                    dve.wait_ge(exp_done, head + h + 1)
                    for n, (lo, hi) in enumerate(((0, P), (P, 3 * P))):
                        last = nc.vector.scalar_tensor_tensor(out=pr[:, h, lo:hi], in0=pr[:, h, lo:hi], scalar=1.0,
                                                              in1=count[:, lo:hi], op0=ALU.mult, op1=ALU.mult,
                                                              accum_out=denom[:, h, n:n + 1])
                    link(last)
                    link(nc.vector.reciprocal(rdenom[:, h, :], denom[:, h, :]))
                    nc.vector.tensor_scalar(pr[:, h, 0:P], pr[:, h, 0:P], rdenom[:, h, 0:1], None, ALU.mult)
                    nc.vector.tensor_scalar(pr[:, h, P:3 * P], pr[:, h, P:3 * P], rdenom[:, h, 1:2], None,
                                            ALU.mult).then_inc(p_ready, 1)

                def y_rest(h):
                    dve.wait_ge(y_hi, head + h + 1)
                    nc.vector.tensor_tensor(bufb_lo[:, ds(head + h, 1), :], head_bank(h)[:, 0:SEQ].rearrange("p (k t) -> p k t", k=1),
                                            bufb_hi[:, ds(head + h, 1), :].bitcast(F32), ALU.subtract).then_inc(y_lo, 1)

                split(q, 4, 12)
                block_out(q, turn, 1)
                split(k, 4, 6)
                dve.wait_ge(scores_done, FREE + head)
                turn_copy(turn, q_t)
                split(k, 6, 12)
                block_out(k, turn + 1, 0)
                split(v, 4, 6)
                turn_copy(turn + 1, k_t)
                split(v, 6, 9)
                bias_and_max(0)
                split(v, 9, 10)
                bias_and_max(1)
                normalise(0)
                split(v, 10, 11)
                bias_and_max(2)
                split(v, 11, 12)
                acc_done(v)
                dve.wait_ge(pv_done, FREE + head)
                nc.vector.tensor_scalar(v_n[:, 1, :], acc[pair(v)][1][:, :], rnorm[:, 0, 1:2], None,
                                        ALU.mult).then_inc(acc_free[pair(v)][1], 1)
                bias_and_max(3)
                normalise(1)
                split(ga, 4, 5)
                normalise(2)
                split(ga, 5, 6)
                normalise(3)
                split(ga, 6, 9)
                y_rest(0)
                split(ga, 9, 10)
                y_rest(1)
                split(ga, 10, 11)
                y_rest(2)
                split(ga, 11, 12)
                y_rest(3)
                chain.leave(COLS)

            for b in range(TB):
                dve.wait_ge(acc_free[1][b], FREE + U_PATT // 2)
            for c in range(COLS):
                unit = (U_PATT + c, 0, 0)
                split(unit, 4, 6)
                if c:
                    turn_lo(T_MERGE + c - 1, bufa_lo, bufa_hi, HC * (c - 1), scale=0.5)
                split(unit, 6, 12)
                acc_done(unit)
                dve.wait_ge(pe_turned, 2 * (T_MERGE + c))
                for b in range(TB):
                    nc.vector.scalar_tensor_tensor(out=block_n[:, b, :], in0=gate_a[:, b, c * NC:(c + 1) * NC], scalar=1.0,
                                                   in1=acc[pair(unit)][b][:, :], op0=ALU.add,
                                                   op1=ALU.mult).then_inc(acc_free[pair(unit)][b], 1)
                for b in range(TB):
                    dve.wait_ge(acc_free[pair(unit)][b], read_out(unit))
                    last = nc.vector.tensor_tensor(block_n[:, b, :], block_n[:, b, :], merged[:, b, c * NC:(c + 1) * NC], ALU.add)
                last.then_inc(block_ready, 1)

            def add_to_resid(unit, n):
                acc_done(unit)
                for b in range(TB):
                    part = resid[:, b, n * NC:(n + 1) * NC]
                    nc.vector.tensor_tensor(part, part, acc[pair(unit)][b][:, :], ALU.add).then_inc(acc_free[pair(unit)][b], 1)

            for c in range(COLS):
                unit = (U_OUT + c, 0, 0)
                split(unit, 4, 6)
                if c == 0:
                    turn_lo(T_H - 1, bufa_lo, bufa_hi, HC * (COLS - 1), scale=0.5)
                else:
                    turn_lo(T_H + c - 1, bufb_lo, bufb_hi, HC * (c - 1), gain=COL["norm_mlp_g"])
                split(unit, 6, 12)
                add_to_resid(unit, c)

            def group(unit0, turn0, first=False, last=False):
                base, i, per = unit0
                for n in range(COLS):
                    unit = (base + n, i, per)
                    split(unit, 4, 6)
                    if n:
                        turn_lo(turn0 + (n - 1), bufa_lo, bufa_hi, HC * (n - 1))
                        split(unit, 6, 12)
                    elif first:
                        turn_lo(T_HID - 1, bufb_lo, bufb_hi, HC * (COLS - 1), gain=COL["norm_mlp_g"])
                        variance(TB + TB * COLS, sumsq[:, 1, :].rearrange("p (b c) -> p b c", c=COLS))
                        split(unit, 6, 8)
                        rsqrt(2, rnorm[:, 3, :]).then_inc(rnorm_ready, 1)
                        split(unit, 8, 12)
                    else:
                        split(unit, 6, 12)
                    for b in range(TB):
                        dve.wait_ge(acc_free[pair(unit)][b], read_out(unit))
                        last_sq = nc.vector.tensor_tensor(block_n[:, b, :], block_n[:, b, :], block_n[:, b, :], ALU.mult)
                    last_sq.then_inc(block_ready, 1)
                for n in range(COLS):
                    unit = (base + COLS + n, i, per)
                    split(unit, 4, 6)
                    if n == 0:
                        turn_lo(turn0 + (COLS - 1), bufa_lo, bufa_hi, HC * (COLS - 1))
                    split(unit, 6, 8 if last and n == COLS - 1 else 12)
                    add_to_resid(unit, n)

            mlp_groups(dve, group)

            variance(TB + 2 * TB * COLS, sumsq[:, 0, :].rearrange("p (b c) -> p b c", c=COLS))
            link(rsqrt(3, rnorm[:, 4, :]))
            dve.wait_ge(gf_landed, 16)
            for c in range(COLS):
                for b in range(TB):
                    part = resid[:, b, c * NC:(c + 1) * NC]
                    fin = nc.vector.scalar_tensor_tensor(out=part, in0=part, scalar=rnorm[:, 4, b:b + 1],
                                                         in1=merged[:, 0, c * NC:(c + 1) * NC], op0=ALU.mult, op1=ALU.mult)
                fin.then_inc(final_ready, 1)


_INS = ["x", "norm_mix_g", "w_in", "conv_w", "conv_b", "lru_wa", "lru_ba", "lru_wx", "lru_bx", "lru_lambda",
        "w_proj_attn", "w_proj_lru", "w_out", "norm_mlp_g", "w_up", "w_down", "norm_final_g"]


def kernel(**inputs):
    import numpy as _np
    import concourse.bacc as _bacc
    from concourse.bass_utils import run_bass_kernel_spmd as _run

    nc = _bacc.Bacc("TRN2", target_bir_lowering=False, num_devices=1)
    arrays, args = {}, []
    for name in _INS:
        a = _np.ascontiguousarray(inputs[name])
        arrays[f"in_{name}"] = a
        args.append(nc.dram_tensor(f"in_{name}", a.shape, mybir.dt.from_np(a.dtype), kind="ExternalInput").ap())
    args.append(nc.dram_tensor("out", (1, SEQ, D), F32, kind="ExternalOutput").ap())
    build(nc, *args)
    r = _run(nc, [arrays], core_ids=[0])
    return r.results[0]["out"]
```

```python
from contextlib import ExitStack

import concourse.bass as bass
from concourse import mybir

F32 = mybir.dt.float32
F32R = mybir.dt.float32r
I32 = mybir.dt.int32
ALU = mybir.AluOpType
ACT = mybir.ActivationFunctionType
AX_X = mybir.AxisListType.X
ds = bass.ds

P = 128
SEQ = 256
TB = SEQ // P
D = 2048
KT = D // P
NC = 512
COLS = D // NC
HC = NC // P
CHUNKS = 8
CK = KT // CHUNKS
RING = 4
F = 4 * D
GROUPS = F // D
CONV_W = 4
PAD = CONV_W - 1
HEADS = 16
QK_SCALE = float(P) ** -0.5
LRU_C = 8.0
EPS = 1e-6
MASKED = -1e30

U_LRU = 0
U_PLRU = U_LRU + 3 * COLS
U_ATT = U_PLRU + COLS
U_PATT = U_ATT + 4 * COLS
U_OUT = U_PATT + COLS
U_MLP = U_OUT + COLS

T_X = 0
T_LRU = T_X + COLS
T_ATT = T_LRU + 2 * COLS
T_MERGE = T_ATT + 2 * COLS
T_H = T_MERGE + COLS
T_HID = T_H + COLS

SCRATCH = 3 * HC * SEQ + (HC + 2) * 3 * P

ROWS = ["conv0", "conv1", "conv2", "conv3", "norm_mlp_g", "conv_b", "lru_ba", "lru_bx", "lru_lambda"]
COL = {name: KT * n for n, name in enumerate(ROWS)}

SPLIT_CREDIT = CHUNKS
FREE = 1


class Chain:

    def __init__(self, eng, sem):
        self.eng, self.sem, self.n, self.offset = eng, sem, 0, 0

    def link(self, instruction):
        self.n += 1
        instruction.then_inc(self.sem, 1)
        self.eng.wait_ge(self.sem, self.n + self.offset)

    def enter(self, i, per):
        self.start, self.per, self.offset = self.n, per, i * per

    def leave(self, iterations):
        assert self.n - self.start == self.per, (self.n - self.start, self.per)
        self.n, self.offset = self.start + self.per * iterations, 0


def build(nc, x, norm_mix_g, w_in, conv_w, conv_b, lru_wa, lru_ba, lru_wx, lru_bx, lru_lambda,
          w_proj_attn, w_proj_lru, w_out, norm_mlp_g, w_up, w_down, norm_final_g, out):
    with ExitStack() as ctx:
        def sb(name, shape, dt=F32):
            return ctx.enter_context(nc.sbuf_tensor(name, shape, dt))

        def sem(name):
            return ctx.enter_context(nc.semaphore(name))

        raw = sb("raw", [P, CHUNKS, CK, NC])
        w_hi = sb("w_hi", [P, RING, CK, NC], F32R)
        w_lo = sb("w_lo", [P, RING, CK, NC], F32R)
        bufa_hi = sb("bufa_hi", [P, KT, SEQ], F32R)
        bufa_lo = sb("bufa_lo", [P, KT, SEQ], F32R)
        bufb_hi = sb("bufb_hi", [P, KT, SEQ], F32R)
        bufb_lo = sb("bufb_lo", [P, KT, SEQ], F32R)
        resid = sb("resid", [P, TB, D])
        merged = sb("merged", [P, TB, D])
        gate_a = sb("gate_a", [P, TB, D])
        block_n = sb("block_n", [P, TB, NC])
        scratch = sb("scratch", [P, SCRATCH])
        ident = sb("ident", [P, P])
        dist = sb("dist", [P, 3 * P])
        count = sb("count", [P, 3 * P])
        gain_rows = sb("gain_rows", [KT, P])
        mix_gain = sb("mix_gain", [P, KT])
        prm_rows = sb("prm_rows", [P, 2, P])
        prm = sb("prm", [P, len(ROWS) * KT])
        neg_ba = sb("neg_ba", [P, KT])
        half_bx = sb("half_bx", [P, KT])
        c_sp = sb("c_sp", [P, 2, KT])
        small = sb("small", [P, 5, KT])
        slopes = sb("slopes", [P, HEADS])
        sumsq = sb("sumsq", [P, 2, TB * COLS])
        rnorm = sb("rnorm", [P, 5, TB])
        rtmp = sb("rtmp", [P, 4, TB])
        negmax = sb("negmax", [P, HC, 2])
        denom = sb("denom", [P, HC, 2])
        rdenom = sb("rdenom", [P, HC, 2])

        tile = HC * SEQ
        ROW = SEQ + 8
        xr_pad = scratch[:, 0:HC * ROW].rearrange("p (b t) -> p b t", b=HC)

        def lru_tile(n):
            a = HC * ROW + n * tile
            return scratch[:, a:a + tile].rearrange("p (b t) -> p b t", b=HC)

        xc, rr, aa, ti = (lru_tile(n) for n in range(4))
        a_sq = scratch[:, 0:tile].rearrange("p (b t) -> p b t", b=HC)
        gate_w = gate_a[:, 0, :].rearrange("p (h b g j) -> p h b g j", h=2, b=HC, g=2)
        q_t = scratch[:, 0:tile].rearrange("p (h t) -> p h t", h=HC)
        k_t = scratch[:, tile:2 * tile].rearrange("p (h t) -> p h t", h=HC)
        v_n = scratch[:, 2 * tile:3 * tile].rearrange("p (b n) -> p b n", b=TB)
        pr = scratch[:, 3 * tile:3 * tile + HC * 3 * P].rearrange("p (h s) -> p h s", h=HC)
        pr_t = scratch[:, 3 * tile + HC * 3 * P:SCRATCH].rearrange("p (h s) -> p h s", h=2)
        dist_i = scratch[:, 0:3 * P].bitcast(I32)
        bits_i = scratch[:, 3 * P:6 * P].bitcast(I32)
        mask_a, mask_b, mask_c = (scratch[:, n * 3 * P:(n + 1) * 3 * P] for n in (2, 3, 4))

        acc = [[ctx.enter_context(nc.psum_tensor(f"acc{p}{t}", [P, NC], F32)) for t in range(TB)] for p in range(2)]
        aux = [ctx.enter_context(nc.psum_tensor(f"aux{n}", [P, NC], F32)) for n in range(4)]

        mlp_gain = prm[:, COL["norm_mlp_g"]:COL["norm_mlp_g"] + KT]

        def head_bank(h):
            return aux[(2 + h) % 4]

        raw_landed = [sem(f"raw_landed{j}") for j in range(CHUNKS)]
        hi_ready, lo_ready, chunks_multiplied = sem("hi_ready"), sem("lo_ready"), sem("chunks_multiplied")
        acc_free = [[sem(f"acc_free{p}{t}") for t in range(TB)] for p in range(2)]
        x_landed = [sem(f"x_landed{c}") for c in range(COLS)]
        gain_landed, gain_turned, gain_ready = sem("gain_landed"), sem("gain_turned"), sem("gain_ready")
        prm_landed, gf_landed, gate_w_landed, stored = sem("prm_landed"), sem("gf_landed"), sem("gate_w_landed"), sem("stored")
        id_zero, id_ready, iota_ready, slopes_ready, masks_ready = (
            sem(n) for n in ("id_zero", "id_ready", "iota_ready", "slopes_ready", "masks_ready"))
        prm_turned, prm_ready, abs_ready, exp_l_ready, lru_prm_ready = (
            sem(n) for n in ("prm_turned", "prm_ready", "abs_ready", "exp_l_ready", "lru_prm_ready"))
        squares_ready, var_ready, root_ready, rnorm_ready = (
            sem(n) for n in ("squares_ready", "var_ready", "root_ready", "rnorm_ready"))
        block_ready, pe_turned, turned_act, turned_dve = (sem(n) for n in ("block_ready", "pe_turned", "turned_act", "turned_dve"))
        conv_begun, xc_ready, gates_done, gates_read, r_ready, a_ready = (
            sem(n) for n in ("conv_begun", "xc_ready", "gates_done", "gates_read", "r_ready", "a_ready"))
        a_sq_ready, m2_ready, root_gelu, lru_y, lru_y_hi, lru_y_lo = (
            sem(n) for n in ("a_sq_ready", "m2_ready", "root_gelu", "lru_y", "lru_y_hi", "lru_y_lo"))
        scores_done, max_ready, exp_done, p_ready, pt_done, pt_read, pv_done, y_hi, y_lo = (
            sem(n) for n in ("scores_done", "max_ready", "exp_done", "p_ready", "pt_done", "pt_read", "pv_done", "y_hi", "y_lo"))
        gained, final_act, final_dve = sem("gained"), sem("final_act"), sem("final_dve")
        shares_ready = sem("shares_ready")
        dve_chain, pool_chain = sem("dve_chain"), sem("pool_chain")

        Q, K, V, XR, XG, GA, GL = (n * D for n in range(7))

        def value(unit, per_unit, add):
            base, i, per = unit
            return per_unit * base + add + i * (per_unit * per)

        def pair(unit):
            return unit[0] % 2

        def read_out(unit):
            base, i, per = unit
            assert per % 2 == 0
            return FREE + base // 2 + 1 + i * (per // 2)

        def mlp_groups(eng, group):
            group((U_MLP, 0, 0), T_HID, first=True)
            with eng.Fori(0, GROUPS - 2) as i:
                group((U_MLP + 2 * COLS, i, 2 * COLS), T_HID + COLS + i * COLS)
            group((U_MLP + 2 * COLS * (GROUPS - 1), 0, 0), T_HID + COLS * (GROUPS - 1), last=True)

        block = ctx.enter_context(nc.Block())

        @block.sync
        def _(sp):
            def load_unit(unit, w, row, col):
                for j in range(CHUNKS):
                    sp.wait_ge(lo_ready, value(unit, CHUNKS, j + 1))
                    src = w[ds(row + j * CK * P, CK * P), ds(col, NC)].rearrange("(k p) n -> p k n", p=P)
                    sp.dma_start(raw[:, j], src).then_inc(raw_landed[j], 16)

            xv = x[0].rearrange("(b p) n -> p b n", p=P)
            for c in range(COLS):
                sp.dma_start(resid[:, :, c * NC:(c + 1) * NC], xv[:, :, c * NC:(c + 1) * NC]).then_inc(x_landed[c], 16)
            with sp.Fori(0, COLS // 2) as i:
                for half in range(2):
                    for n, part in enumerate((XR, XG, GL)):
                        load_unit((U_LRU + 3 * half + n, i, 6), w_in[0], 0, part + half * NC + i * (2 * NC))
                        if half == 0 and n == 0:
                            sp.wait_ge(gates_done, FREE + i * (2 * HC))
                            for hh in range(2):
                                for g, w in enumerate((lru_wa, lru_wx)):
                                    src = w[0, ds(i * (2 * HC) + hh * HC, HC)].rearrange("b i j -> i b j")
                                    sp.dma_start(gate_w[:, hh, :, g, :], src).then_inc(gate_w_landed, 16)
            with sp.Fori(0, COLS // 2) as i:
                for n in range(2):
                    load_unit((U_PLRU + n, i, 2), w_proj_lru[0], 0, n * NC + i * (2 * NC))
            with sp.Fori(0, COLS) as i:
                for n, part in enumerate((Q, K, V, GA)):
                    load_unit((U_ATT + n, i, 4), w_in[0], 0, part + i * NC)
            for c in range(COLS):
                load_unit((U_PATT + c, 0, 0), w_proj_attn[0], 0, c * NC)
            for c in range(COLS):
                load_unit((U_OUT + c, 0, 0), w_out[0], 0, c * NC)
            sp.wait_ge(block_ready, COLS)
            sp.dma_start(merged[:, 0, :], norm_final_g.rearrange("(a n) -> a n", a=1).broadcast_to([P, D])).then_inc(gf_landed, 16)
            with sp.Fori(0, GROUPS) as i:
                for n in range(COLS):
                    load_unit((U_MLP + n, i, 2 * COLS), w_up[0], 0, n * NC + i * D)
                for n in range(COLS):
                    load_unit((U_MLP + COLS + n, i, 2 * COLS), w_down[0], i * D, n * NC)
            ov = out[0].rearrange("(b p) n -> p b n", p=P)
            for c in range(COLS):
                sp.wait_ge(final_act, c + 1)
                sp.wait_ge(final_dve, c + 1)
                sp.dma_start(ov[:, :, c * NC:(c + 1) * NC], resid[:, :, c * NC:(c + 1) * NC]).then_inc(stored, 16)
            sp.wait_ge(stored, 16 * COLS)

        @block.gpsimd
        def _(pool):
            for buffer_free in (gates_done, gates_read, lru_y_lo, scores_done, pv_done, m2_ready, pt_done, y_lo,
                                *acc_free[0], *acc_free[1]):
                pool.sem_inc(buffer_free, FREE)
            nc.gpsimd.memset(ident[:, :], 0.0).then_inc(id_zero, 1)
            pool.wait_ge(id_zero, 1)
            nc.gpsimd.affine_select(out=ident[:, :], in_=ident[:, :], compare_op=ALU.not_equal, fill=1.0,
                                    base=0, pattern=[[-1, P]], channel_multiplier=1).then_inc(id_ready, 1)
            pool.dma_start(prm_rows[0:CONV_W * KT, 0, :], conv_w[0].rearrange("w (k p) -> (w k) p", p=P)).then_inc(prm_landed, 16)
            for n, src in enumerate((norm_mlp_g, conv_b, lru_ba, lru_bx, lru_lambda)):
                r = (CONV_W + n) * KT
                pool.dma_start(prm_rows[r % P:r % P + KT, r // P, :],
                               src[0].rearrange("(k p) -> k p", p=P)).then_inc(prm_landed, 16)
            for h in range(HEADS):
                last = nc.gpsimd.memset(slopes[:, h:h + 1], 2.0 ** (-8.0 * (h + 1) / HEADS))
            last.then_inc(slopes_ready, 1)

            link = Chain(pool, pool_chain).link
            e, s, s2, p = (small[:, n, :] for n in (1, 2, 3, 4))
            pool.wait_ge(shares_ready, 1)
            link(nc.gpsimd.tensor_tensor(s, s, e, ALU.mult))
            link(nc.gpsimd.tensor_tensor(s2, s, s, ALU.mult))
            link(nc.gpsimd.tensor_scalar(p, s2, 1.0 / 15, 1.0 / 13, ALU.mult, ALU.add))
            for odd in (11, 9, 7, 5, 3, 1):
                link(nc.gpsimd.tensor_tensor(p, p, s2, ALU.mult))
                link(nc.gpsimd.tensor_scalar(p, p, 1.0 / odd, None, ALU.add))
            link(nc.gpsimd.tensor_tensor(p, p, s, ALU.mult))
            lam = prm[:, COL["lru_lambda"]:COL["lru_lambda"] + KT]
            link(nc.gpsimd.tensor_scalar(s, lam, -1.0, 0.0, ALU.mult, ALU.max))
            link(nc.gpsimd.tensor_scalar(p, p, 2.0, None, ALU.mult))
            link(nc.gpsimd.tensor_tensor(p, p, s, ALU.add))
            nc.gpsimd.tensor_scalar(c_sp[:, 0, :], p, -LRU_C, None, ALU.mult)
            nc.gpsimd.tensor_scalar(c_sp[:, 1, :], p, LRU_C, None, ALU.mult)
            nc.gpsimd.tensor_scalar(neg_ba[:, :], prm[:, COL["lru_ba"]:COL["lru_ba"] + KT], -1.0, None, ALU.mult)
            nc.gpsimd.tensor_scalar(half_bx[:, :], prm[:, COL["lru_bx"]:COL["lru_bx"] + KT], 0.5, None,
                                    ALU.mult).then_inc(lru_prm_ready, 1)
            with pool.Fori(0, COLS) as c:
                pool.wait_ge(a_ready, c + 1)
                nc.gpsimd.tensor_tensor(a_sq, aa, aa, ALU.mult).then_inc(a_sq_ready, 1)
            pool.wait_ge(lru_y_lo, FREE + COLS)
            for n, base in enumerate((0, P, 0)):
                nc.gpsimd.iota(dist_i[:, n * P:(n + 1) * P], pattern=[[-1, P]], base=base,
                               channel_multiplier=1).then_inc(iota_ready, 1)

        @block.tensor
        def _(pe):
            def chunks(unit, first, last, hi, lo):
                for j in range(first, last):
                    pe.wait_ge(lo_ready, value(unit, CHUNKS, j + 1 + SPLIT_CREDIT))
                    for b in range(TB):
                        if j == 0:
                            pe.wait_ge(acc_free[pair(unit)][b], read_out(unit) - 1)
                        for kk in range(CK):
                            k = j * CK + kk
                            a_hi, a_lo = hi[:, k, b * P:(b + 1) * P], lo[:, k, b * P:(b + 1) * P]
                            b_hi, b_lo = w_hi[:, j % RING, kk, :], w_lo[:, j % RING, kk, :]
                            dst = acc[pair(unit)][b][:, :]
                            nc.tensor.matmul(dst, a_hi, b_hi, start=k == 0, stop=False)
                            nc.tensor.matmul(dst, a_hi, b_lo, start=False, stop=False)
                            mm = nc.tensor.matmul(dst, a_lo, b_hi, start=False, stop=k == KT - 1)
                    mm.then_inc(chunks_multiplied, 1)

            def turn(number, src, dve_reads, bank0=0):
                for b in range(2):
                    if dve_reads is not None:
                        pe.wait_ge(turned_act, number * 2 + b - 1)
                        pe.wait_ge(turned_dve, dve_reads + b - 1)
                    for k in range(2):
                        for t in range(TB):
                            tr = nc.tensor.transpose(aux[bank0 + b][:, k * SEQ + t * P:k * SEQ + (t + 1) * P],
                                                     src[:, t, (2 * b + k) * P:(2 * b + k + 1) * P], ident[:, :])
                    tr.then_inc(pe_turned, 1)

            def block_turn(number, unit, dve_reads):
                for b in range(TB):
                    pe.wait_ge(acc_free[pair(unit)][b], read_out(unit))
                turn(number, block_n, dve_reads)

            A, B = (bufa_hi, bufa_lo), (bufb_hi, bufb_lo)

            pe.wait_ge(id_ready, 1)
            pe.wait_ge(gain_landed, 16)
            nc.tensor.transpose(acc[1][0][:, 0:KT], gain_rows[:, :], ident[0:KT, 0:KT]).then_inc(gain_turned, 1)
            for c in range(COLS):
                pe.wait_ge(x_landed[c], 16)
                if c >= 2:
                    pe.wait_ge(turned_dve, 2 * (c - 1))
                turn(T_X + c, resid[:, :, c * NC:(c + 1) * NC], None, bank0=2 * (c % 2))
            pe.wait_ge(prm_landed, 16 * (len(ROWS) - CONV_W + 1))
            nc.tensor.transpose(acc[1][1][:, 0:P], prm_rows[:, 0, :], ident[:, :])
            rest = len(ROWS) * KT - P
            nc.tensor.transpose(acc[1][1][:, P:P + rest], prm_rows[0:rest, 1, :], ident[0:rest, 0:rest]).then_inc(prm_turned, 1)

            with pe.Fori(0, COLS // 2) as i:
                for half in range(2):
                    xr, xg, gl = ((U_LRU + 3 * half + n, i, 6) for n in range(3))
                    turn_xr = T_LRU + 2 * half + i * 4
                    blk = half * HC + i * (2 * HC)
                    dve_reads = 2 * T_LRU + 2 * half + i * 4
                    for c in range(COLS):
                        pe.wait_ge(turned_dve, 2 * (c + 1))
                        chunks(xr, 2 * c, 2 * c + 2, *A)
                    chunks(xg, 0, 1, *A)
                    block_turn(turn_xr, xr, dve_reads)
                    chunks(xg, 1, 6, *A)
                    if half == 0:
                        pe.wait_ge(gate_w_landed, 64 + i * 64)
                    for b in range(HC):
                        pe.wait_ge(xc_ready, blk + b + 1)
                        pe.wait_ge(gates_read, FREE + blk + max(b - 1, 0))
                        for g in range(2):
                            mm = nc.tensor.matmul(aux[2 + b % 2][:, g * SEQ:(g + 1) * SEQ], gate_w[:, half, b, g, :],
                                                  xc[:, b, :], start=True, stop=True)
                        mm.then_inc(gates_done, 1)
                        if b % 2:
                            chunks(xg, 6 + b // 2, 7 + b // 2, *A)
                    chunks(gl, 0, 2, *A)
                    block_turn(turn_xr + 1, xg, dve_reads + 2)
                    chunks(gl, 2, 8, *A)

            pe.wait_ge(lru_y_lo, FREE + COLS - 1)
            with pe.Fori(0, COLS // 2) as i:
                for n in range(2):
                    chunks((U_PLRU + n, i, 2), 0, 6, *B)
                    if n == 0:
                        pe.wait_ge(lru_y_lo, FREE + COLS)
                    chunks((U_PLRU + n, i, 2), 6, 8, *B)

            with pe.Fori(0, COLS) as i:
                q, k, v, ga = ((U_ATT + n, i, 4) for n in range(4))
                turn_q = T_ATT + i * 2
                dve_reads = 2 * T_LRU + 2 * COLS + i * 4
                head = i * HC
                chunks(q, 0, 8, *A)
                chunks(k, 0, 1, *A)
                pe.wait_ge(y_lo, FREE + head)
                block_turn(turn_q, q, dve_reads)
                chunks(k, 1, 8, *A)
                chunks(v, 0, 1, *A)
                block_turn(turn_q + 1, k, dve_reads + 2)
                chunks(v, 1, 3, *A)
                pe.wait_ge(turned_act, turn_q * 2 + 4)
                pe.wait_ge(turned_dve, dve_reads + 4)
                for h in range(HC):
                    nc.tensor.matmul(head_bank(h)[:, 0:P], q_t[:, h, 0:P], k_t[:, h, 0:P], start=True, stop=True)
                    nc.tensor.matmul(head_bank(h)[:, P:3 * P], q_t[:, h, P:SEQ], k_t[:, h, :], start=True,
                                     stop=True).then_inc(scores_done, 1)
                    if h == 1:
                        chunks(v, 3, 4, *A)
                chunks(v, 4, 8, *A)

                def turn_probs(h):
                    pe.wait_ge(p_ready, head + h + 1)
                    for n in range(3):
                        tr = nc.tensor.transpose(head_bank(h)[:, n * P:(n + 1) * P], pr[:, h, n * P:(n + 1) * P], ident[:, :])
                    tr.then_inc(pt_done, 1)

                def times_values(h):
                    pe.wait_ge(pt_read, head + h + 1)
                    for b in range(TB):
                        pe.wait_ge(acc_free[pair(v)][b], read_out(v))
                    dst = head_bank(h)
                    nc.tensor.matmul(dst[:, 0:SEQ], v_n[:, 0, h * P:(h + 1) * P], pr_t[:, h % 2, 0:2 * P], start=True,
                                     stop=False, skip_group_check=True)
                    nc.tensor.matmul(dst[:, P:SEQ], v_n[:, 1, h * P:(h + 1) * P], pr_t[:, h % 2, 2 * P:3 * P], start=False,
                                     stop=True, skip_group_check=True).then_inc(pv_done, 1)

                turn_probs(0)
                chunks(ga, 0, 1, *A)
                turn_probs(1)
                chunks(ga, 1, 2, *A)
                times_values(0)
                chunks(ga, 2, 3, *A)
                times_values(1)
                turn_probs(2)
                chunks(ga, 3, 4, *A)
                turn_probs(3)
                chunks(ga, 4, 5, *A)
                times_values(2)
                chunks(ga, 5, 6, *A)
                times_values(3)
                chunks(ga, 6, 8, *A)

            dve0 = 2 * T_LRU + 2 * COLS - 2 * T_ATT
            pe.wait_ge(y_lo, FREE + HEADS - HC)
            for c in range(COLS):
                unit = (U_PATT + c, 0, 0)
                chunks(unit, 0, 1, *B)
                if c:
                    pe.wait_ge(block_ready, c)
                    turn(T_MERGE + c - 1, block_n, 2 * (T_MERGE + c - 1) + dve0)
                chunks(unit, 1, 6, *B)
                if c == 0:
                    pe.wait_ge(y_lo, FREE + HEADS)
                chunks(unit, 6, 8, *B)

            for c in range(COLS):
                unit = (U_OUT + c, 0, 0)
                if c == 0:
                    pe.wait_ge(turned_dve, 2 * (T_H - 1) + dve0)
                chunks(unit, 0, 1, *A)
                if c == 0:
                    pe.wait_ge(block_ready, COLS)
                    turn(T_H - 1, block_n, 2 * (T_H - 1) + dve0)
                else:
                    before = (U_OUT + c - 1, 0, 0)
                    for b in range(TB):
                        pe.wait_ge(acc_free[pair(before)][b], read_out(before))
                    turn(T_H + c - 1, resid[:, :, (c - 1) * NC:c * NC], 2 * (T_H + c - 1) + dve0)
                chunks(unit, 1, 6, *A)
                if c == 0:
                    pe.wait_ge(turned_dve, 2 * T_H + dve0)
                chunks(unit, 6, 8, *A)

            def group(unit0, turn0, first=False, last=False):
                base, i, per = unit0
                for n in range(COLS):
                    unit = (base + n, i, per)
                    if first and n == 0:
                        pe.wait_ge(turned_dve, 2 * (T_HID - 1) + dve0)
                    chunks(unit, 0, 1, *B)
                    if n:
                        pe.wait_ge(block_ready, turn0 + (n - T_HID + COLS))
                        turn(turn0 + (n - 1), block_n, turn0 * 2 + (2 * (n - 1) + dve0))
                    elif first:
                        before = (U_MLP - 1, 0, 0)
                        for b in range(TB):
                            pe.wait_ge(acc_free[pair(before)][b], read_out(before))
                        turn(T_HID - 1, resid[:, :, D - NC:D], 2 * (T_HID - 1) + dve0)
                    chunks(unit, 1, 6, *B)
                    if first and n == 0:
                        pe.wait_ge(turned_dve, 2 * T_HID + dve0)
                    chunks(unit, 6, 8, *B)
                for n in range(COLS):
                    unit = (base + COLS + n, i, per)
                    if n == 0:
                        pe.wait_ge(turned_dve, turn0 * 2 + (2 * (COLS - 1) + dve0))
                    chunks(unit, 0, 1, *A)
                    if n == 0:
                        pe.wait_ge(block_ready, turn0 + (2 * COLS - T_HID))
                        turn(turn0 + (COLS - 1), block_n, turn0 * 2 + (2 * (COLS - 1) + dve0))
                    chunks(unit, 1, 6, *A)
                    if n == 0:
                        pe.wait_ge(turned_dve, turn0 * 2 + (2 * COLS + dve0))
                    chunks(unit, 6, 8, *A)

            mlp_groups(pe, group)

        @block.scalar
        def _(act):
            def cast(unit, first, last):
                for ch in range(first, last):
                    j = ch % CHUNKS
                    act.wait_ge(raw_landed[j], value(unit, 16, 16 * (ch // CHUNKS + 1)))
                    if ch >= RING:
                        act.wait_ge(chunks_multiplied, value(unit, CHUNKS, ch - RING + 1))
                    nc.scalar.activation(w_hi[:, j % RING], raw[:, j], ACT.Copy).then_inc(hi_ready, 1)

            def acc_done(unit):
                act.wait_ge(chunks_multiplied, value(unit, CHUNKS, CHUNKS))

            def block_out(unit, turn, factor):
                acc_done(unit)
                act.wait_ge(rnorm_ready, 1)
                act.wait_ge(pe_turned, turn * 2)
                nc.scalar.activation(block_n[:, 0, :], acc[pair(unit)][0][:, :], ACT.Copy,
                                     scale=rnorm[:, factor, 0:1]).then_inc(acc_free[pair(unit)][0], 1)

            def turn_hi(turn, dst, tile0, scale=1.0, gain=None, bank0=0):
                for b in range(2):
                    act.wait_ge(pe_turned, turn * 2 + b + 1)
                    if gain is None:
                        n = tile0 + 2 * b
                        nc.scalar.activation(dst[:, n:n + 2, :], aux[b][:, :].rearrange("p (k t) -> p k t", k=2),
                                             ACT.Copy, scale=scale).then_inc(turned_act, 1)
                    else:
                        for k in range(2):
                            n = tile0 + 2 * b + k
                            last = nc.scalar.activation(dst[:, n, :], aux[bank0 + b][:, k * SEQ:(k + 1) * SEQ], ACT.Copy,
                                                        scale=gain[:, n:n + 1])
                        last.then_inc(turned_act, 1)

            def turn_copy(turn, dst):
                act.wait_ge(pe_turned, turn * 2 + 1)
                nc.scalar.activation(dst[:, 0:2], aux[0][:, :].rearrange("p (k t) -> p k t", k=2), ACT.Copy).then_inc(turned_act, 2)

            def root(n):
                act.wait_ge(var_ready, n)
                nc.scalar.activation(rtmp[:, 1, :], rtmp[:, 0, :], ACT.Sqrt).then_inc(root_ready, 1)

            act.dma_start(gain_rows[:, :], norm_mix_g[0].rearrange("(k p) -> k p", p=P)).then_inc(gain_landed, 16)
            act.wait_ge(gain_ready, 1)
            for c in range(COLS):
                turn_hi(T_X + c, bufa_hi, HC * c, gain=mix_gain, bank0=2 * (c % 2))
                cast((0, 0, 0), c, c + 1)
            for b in range(TB):
                nc.scalar.activation(merged[:, b, :], resid[:, b, :], ACT.Square,
                                     accum_out=sumsq[:, 0, b:b + 1]).then_inc(squares_ready, 1)
            act.wait_ge(prm_ready, 1)
            nc.scalar.activation(small[:, 0, :], prm[:, COL["lru_lambda"]:COL["lru_lambda"] + KT], ACT.Abs).then_inc(abs_ready, 1)
            act.wait_ge(abs_ready, 1)
            nc.scalar.activation(small[:, 1, :], small[:, 0, :], ACT.Exp, scale=-1.0).then_inc(exp_l_ready, 1)
            root(1)

            with act.Fori(0, COLS // 2) as i:
                for half in range(2):
                    xr, xg, gl = ((U_LRU + 3 * half + n, i, 6) for n in range(3))
                    turn = T_LRU + 2 * half + i * 4
                    blk = half * HC + i * (2 * HC)
                    col = half + i * 2
                    cast(xr, 4, 11)
                    block_out(xr, turn, 0)
                    cast(xr, 11, 12)
                    cast(xg, 4, 5)
                    act.wait_ge(lru_y_lo, FREE + col)
                    turn_copy(turn, xr_pad[:, :, 8:ROW])
                    act.wait_ge(turned_act, turn * 2 + 2)
                    act.wait_ge(turned_dve, 2 * T_LRU + 2 + 2 * half + i * 4)
                    for b in range(HC):
                        last = nc.scalar.activation(xc[:, b, :], xr_pad[:, b, 8:ROW], ACT.Identity,
                                                    scale=prm[:, ds(COL["conv3"] + b + blk, 1)],
                                                    bias=prm[:, ds(COL["conv_b"] + b + blk, 1)])
                    last.then_inc(conv_begun, 1)
                    cast(xg, 5, 10)
                    act.wait_ge(lru_prm_ready, 1)
                    for b in range(HC):
                        act.wait_ge(gates_done, FREE + blk + b + 1)
                        nc.scalar.activation(rr[:, b, :], aux[2 + b % 2][:, 0:SEQ], ACT.Exp, scale=-1.0,
                                             bias=neg_ba[:, ds(blk + b, 1)])
                        nc.scalar.activation(ti[:, b, :], aux[2 + b % 2][:, SEQ:2 * SEQ], ACT.Tanh, scale=0.5,
                                             bias=half_bx[:, ds(blk + b, 1)]).then_inc(gates_read, 1)
                        if b == 1:
                            cast(xg, 10, 11)
                    block_out(xg, turn + 1, 0)
                    cast(xg, 11, 12)
                    cast(gl, 4, 6)
                    for b in range(HC):
                        act.wait_ge(r_ready, blk + b + 1)
                        nc.scalar.activation(aa[:, b, :], rr[:, b, :], ACT.Exp, scale=c_sp[:, 0, ds(blk + b, 1)])
                        last = nc.scalar.activation(rr[:, b, :], rr[:, b, :], ACT.Tanh, scale=c_sp[:, 1, ds(blk + b, 1)])
                    last.then_inc(a_ready, 1)
                    cast(gl, 6, 8)
                    act.wait_ge(m2_ready, FREE + col + 1)
                    nc.scalar.activation(rr, rr, ACT.Sqrt).then_inc(root_gelu, 1)
                    for b in range(2):
                        act.wait_ge(pe_turned, turn * 2 + 3 + b)
                        nc.scalar.activation(xc[:, 2 * b:2 * b + 2, :], aux[b][:, :].rearrange("p (k t) -> p k t", k=2),
                                             ACT.Gelu_apprx_tanh).then_inc(turned_act, 1)
                    cast(gl, 8, 11)
                    act.wait_ge(lru_y, col + 1)
                    nc.scalar.activation(bufb_hi[:, ds(blk, HC), :], ti, ACT.Copy).then_inc(lru_y_hi, 1)
                    acc_done(gl)
                    for b in range(TB):
                        nc.scalar.activation(merged[:, b, ds(half * NC + i * (2 * NC), NC)], acc[pair(gl)][b][:, :], ACT.Tanh,
                                             scale=rnorm[:, 2, b:b + 1]).then_inc(acc_free[pair(gl)][b], 1)
                    cast(gl, 11, 12)

            with act.Fori(0, COLS // 2) as i:
                for n in range(2):
                    cast((U_PLRU + n, i, 2), 4, 12)

            with act.Fori(0, COLS) as i:
                q, k, v, ga = ((U_ATT + n, i, 4) for n in range(4))
                turn = T_ATT + i * 2
                head = i * HC

                def exps(h):
                    act.wait_ge(max_ready, head + h + 1)
                    nc.scalar.activation(pr[:, h, 0:P], pr[:, h, 0:P], ACT.Exp, bias=negmax[:, h, 0:1])
                    nc.scalar.activation(pr[:, h, P:3 * P], pr[:, h, P:3 * P], ACT.Exp,
                                         bias=negmax[:, h, 1:2]).then_inc(exp_done, 1)

                def probs_out(h):
                    act.wait_ge(pt_done, FREE + head + h + 1)
                    act.wait_ge(pv_done, FREE + head + max(h - 1, 0))
                    nc.scalar.activation(pr_t[:, h % 2, :], head_bank(h)[:, 0:3 * P], ACT.Copy).then_inc(pt_read, 1)

                def y_out(h):
                    act.wait_ge(pv_done, FREE + head + h + 1)
                    nc.scalar.activation(bufb_hi[:, ds(head + h, 1), :], head_bank(h)[:, 0:SEQ].rearrange("p (k t) -> p k t", k=1),
                                         ACT.Copy).then_inc(y_hi, 1)

                cast(q, 4, 11)
                block_out(q, turn, 1)
                cast(q, 11, 12)
                cast(k, 4, 5)
                act.wait_ge(masks_ready, 1)
                act.wait_ge(scores_done, FREE + head)
                turn_copy(turn, q_t)
                cast(k, 5, 11)
                block_out(k, turn + 1, 0)
                cast(k, 11, 12)
                cast(v, 4, 5)
                turn_copy(turn + 1, k_t)
                cast(v, 5, 9)
                exps(0)
                cast(v, 9, 10)
                exps(1)
                cast(v, 10, 11)
                exps(2)
                acc_done(v)
                act.wait_ge(pv_done, FREE + head)
                nc.scalar.activation(v_n[:, 0, :], acc[pair(v)][0][:, :], ACT.Copy,
                                     scale=rnorm[:, 0, 0:1]).then_inc(acc_free[pair(v)][0], 1)
                cast(v, 11, 12)
                exps(3)
                probs_out(0)
                cast(ga, 4, 5)
                probs_out(1)
                cast(ga, 5, 6)
                y_out(0)
                cast(ga, 6, 7)
                y_out(1)
                probs_out(2)
                cast(ga, 7, 8)
                probs_out(3)
                cast(ga, 8, 9)
                y_out(2)
                cast(ga, 9, 10)
                y_out(3)
                cast(ga, 10, 11)
                acc_done(ga)
                for b in range(TB):
                    nc.scalar.activation(gate_a[:, b, ds(i * NC, NC)], acc[pair(ga)][b][:, :], ACT.Tanh,
                                         scale=rnorm[:, 2, b:b + 1]).then_inc(acc_free[pair(ga)][b], 1)
                cast(ga, 11, 12)

            for c in range(COLS):
                unit = (U_PATT + c, 0, 0)
                cast(unit, 4, 5)
                if c:
                    turn_hi(T_MERGE + c - 1, bufa_hi, HC * (c - 1), scale=0.5)
                cast(unit, 5, 12)

            for c in range(COLS):
                unit = (U_OUT + c, 0, 0)
                cast(unit, 4, 5)
                if c == 0:
                    turn_hi(T_H - 1, bufa_hi, HC * (COLS - 1), scale=0.5)
                else:
                    turn_hi(T_H + c - 1, bufb_hi, HC * (c - 1), gain=mlp_gain)
                cast(unit, 5, 12)
                for b in range(TB):
                    act.wait_ge(acc_free[pair(unit)][b], read_out(unit))
                    nc.scalar.activation(block_n[:, b, :], resid[:, b, c * NC:(c + 1) * NC], ACT.Square,
                                         accum_out=sumsq[:, 1, b * COLS + c:b * COLS + c + 1]).then_inc(squares_ready, 1)

            def group(unit0, turn0, first=False, last=False):
                base, i, per = unit0
                for n in range(COLS):
                    unit = (base + n, i, per)
                    cast(unit, 4, 5)
                    if n:
                        turn_hi(turn0 + (n - 1), bufa_hi, HC * (n - 1))
                    elif first:
                        turn_hi(T_HID - 1, bufb_hi, HC * (COLS - 1), gain=mlp_gain)
                        root(2)
                    cast(unit, 5, 11)
                    acc_done(unit)
                    if first and n == 0:
                        act.wait_ge(rnorm_ready, 2)
                    act.wait_ge(pe_turned, turn0 * 2 + 2 * n)
                    for b in range(TB):
                        nc.scalar.activation(block_n[:, b, :], acc[pair(unit)][b][:, :], ACT.Relu,
                                             scale=rnorm[:, 3, b:b + 1]).then_inc(acc_free[pair(unit)][b], 1)
                    cast(unit, 11, 12)
                for n in range(COLS):
                    unit = (base + COLS + n, i, per)
                    cast(unit, 4, 5)
                    if n == 0:
                        turn_hi(turn0 + (COLS - 1), bufa_hi, HC * (COLS - 1))
                    cast(unit, 5, 8 if last and n == COLS - 1 else 12)
                    if last:
                        for b in range(TB):
                            act.wait_ge(acc_free[pair(unit)][b], read_out(unit))
                            nc.scalar.activation(block_n[:, b, :], resid[:, b, n * NC:(n + 1) * NC], ACT.Square,
                                                 accum_out=sumsq[:, 0, b * COLS + n:b * COLS + n + 1]).then_inc(squares_ready, 1)

            mlp_groups(act, group)
            root(3)
            act.wait_ge(rnorm_ready, 3)
            act.wait_ge(gained, COLS)
            for c in range(COLS):
                part = resid[:, 0, c * NC:(c + 1) * NC]
                nc.scalar.activation(part, part, ACT.Copy, scale=rnorm[:, 4, 0:1]).then_inc(final_act, 1)

        @block.vector
        def _(dve):
            chain = Chain(dve, dve_chain)
            link = chain.link

            def split(unit, first, last):
                for ch in range(first, last):
                    j = ch % CHUNKS
                    dve.wait_ge(hi_ready, value(unit, CHUNKS, ch + 1))
                    nc.vector.tensor_tensor(w_lo[:, j % RING], raw[:, j], w_hi[:, j % RING].bitcast(F32),
                                            ALU.subtract).then_inc(lo_ready, 1)

            def acc_done(unit):
                dve.wait_ge(chunks_multiplied, value(unit, CHUNKS, CHUNKS))

            def block_out(unit, turn, factor):
                acc_done(unit)
                dve.wait_ge(pe_turned, turn * 2)
                nc.vector.tensor_scalar(block_n[:, 1, :], acc[pair(unit)][1][:, :], rnorm[:, factor, 1:2], None,
                                        ALU.mult).then_inc(acc_free[pair(unit)][1], 1)

            def turn_lo(turn, dst_lo, dst_hi, tile0, scale=1.0, gain=None, bank0=0):
                for b in range(2):
                    dve.wait_ge(turned_act, turn * 2 + b + 1)
                    if gain is None:
                        n = tile0 + 2 * b
                        nc.vector.scalar_tensor_tensor(
                            out=dst_lo[:, n:n + 2, :], in0=aux[b][:, :].rearrange("p (k t) -> p k t", k=2), scalar=scale,
                            in1=dst_hi[:, n:n + 2, :].bitcast(F32), op0=ALU.mult, op1=ALU.subtract).then_inc(turned_dve, 1)
                    else:
                        for k in range(2):
                            n = tile0 + 2 * b + k
                            last = nc.vector.scalar_tensor_tensor(
                                out=dst_lo[:, n, :], in0=aux[bank0 + b][:, k * SEQ:(k + 1) * SEQ], scalar=gain[:, n:n + 1],
                                in1=dst_hi[:, n, :].bitcast(F32), op0=ALU.mult, op1=ALU.subtract)
                        last.then_inc(turned_dve, 1)

            def turn_copy(turn, dst):
                dve.wait_ge(pe_turned, turn * 2 + 2)
                nc.vector.tensor_copy(dst[:, 2:4], aux[1][:, :].rearrange("p (k t) -> p k t", k=2)).then_inc(turned_dve, 2)

            def variance(squares, total):
                dve.wait_ge(squares_ready, squares)
                link(nc.vector.tensor_reduce(rtmp[:, 0, :], total, AX_X, ALU.add))
                nc.vector.tensor_scalar(rtmp[:, 0, :], rtmp[:, 0, :], 1.0 / D, EPS, ALU.mult, ALU.add).then_inc(var_ready, 1)

            def rsqrt(n, dst):
                dve.wait_ge(root_ready, n)
                link(nc.vector.reciprocal(rtmp[:, 2, :], rtmp[:, 1, :]))
                link(nc.vector.tensor_tensor(rtmp[:, 2, :], rtmp[:, 0, :], rtmp[:, 2, :], ALU.mult))
                link(nc.vector.tensor_tensor(rtmp[:, 2, :], rtmp[:, 1, :], rtmp[:, 2, :], ALU.add))
                link(nc.vector.tensor_scalar(rtmp[:, 2, :], rtmp[:, 2, :], 0.5, None, ALU.mult))
                return nc.vector.reciprocal(dst, rtmp[:, 2, :])

            nc.vector.memset(rtmp[:, 3, :], 0.0).then_inc(lo_ready, SPLIT_CREDIT)

            dve.wait_ge(gain_turned, 1)
            nc.vector.tensor_copy(mix_gain[:, :], acc[1][0][:, 0:KT]).then_inc(gain_ready, 1)
            dve.wait_ge(gain_ready, 1)
            for c in range(COLS):
                turn_lo(T_X + c, bufa_lo, bufa_hi, HC * c, gain=mix_gain, bank0=2 * (c % 2))
                split((0, 0, 0), c, c + 1)
            dve.wait_ge(prm_turned, 1)
            nc.vector.tensor_copy(prm[:, :], acc[1][1][:, 0:len(ROWS) * KT]).then_inc(prm_ready, 1)
            variance(TB, sumsq[:, 0, 0:TB].rearrange("p (b c) -> p b c", c=1))
            dve.wait_ge(exp_l_ready, 1)
            link(nc.vector.tensor_scalar(small[:, 3, :], small[:, 1, :], 2.0, None, ALU.add))
            nc.vector.reciprocal(small[:, 2, :], small[:, 3, :]).then_inc(shares_ready, 1)
            link(rsqrt(1, rnorm[:, 0, :]))
            nc.vector.tensor_scalar(rnorm[:, 1, :], rnorm[:, 0, :], QK_SCALE, None, ALU.mult)
            nc.vector.tensor_scalar(rnorm[:, 2, :], rnorm[:, 0, :], 0.5, None, ALU.mult).then_inc(rnorm_ready, 1)

            with dve.Fori(0, COLS // 2) as i:
                chain.enter(i, 2 * 10)
                for half in range(2):
                    xr, xg, gl = ((U_LRU + 3 * half + n, i, 6) for n in range(3))
                    turn = T_LRU + 2 * half + i * 4
                    blk = half * HC + i * (2 * HC)
                    col = half + i * 2
                    split(xr, 4, 11)
                    block_out(xr, turn, 0)
                    split(xr, 11, 12)
                    dve.wait_ge(m2_ready, FREE + col)
                    link(nc.vector.memset(xr_pad[:, :, 8 - PAD:8], 0.0))
                    split(xg, 4, 5)
                    turn_copy(turn, xr_pad[:, :, 8:ROW])
                    split(xg, 5, 6)
                    dve.wait_ge(conv_begun, col + 1)
                    for lag in range(1, CONV_W):
                        for b in range(HC):
                            tap = nc.vector.scalar_tensor_tensor(
                                out=xc[:, b, :], in0=xr_pad[:, b, 8 - lag:ROW - lag],
                                scalar=prm[:, ds(COL[f"conv{PAD - lag}"] + b + blk, 1)], in1=xc[:, b, :],
                                op0=ALU.mult, op1=ALU.add)
                            if lag == PAD:
                                tap.then_inc(xc_ready, 1)
                        if lag != PAD:
                            link(tap)
                            split(xg, 5 + lag, 6 + lag)
                    split(xg, 8, 10)
                    for b in range(HC):
                        dve.wait_ge(gates_read, FREE + blk + b + 1)
                        link(nc.vector.tensor_scalar(rr[:, b, :], rr[:, b, :], 1.0, None, ALU.add))
                        nc.vector.reciprocal(rr[:, b, :], rr[:, b, :]).then_inc(r_ready, 1)
                        if b == 1:
                            split(xg, 10, 11)
                    block_out(xg, turn + 1, 0)
                    split(xg, 11, 12)
                    split(gl, 4, 6)
                    link(nc.vector.scalar_tensor_tensor(out=ti, in0=ti, scalar=1.0, in1=xc, op0=ALU.add, op1=ALU.mult))
                    dve.wait_ge(a_sq_ready, col + 1)
                    nc.vector.scalar_tensor_tensor(out=rr, in0=a_sq, scalar=1.0, in1=rr, op0=ALU.add,
                                                   op1=ALU.mult).then_inc(m2_ready, 1)
                    split(gl, 6, 9)
                    dve.wait_ge(root_gelu, col + 1)
                    link(nc.vector.scalar_tensor_tensor(out=ti, in0=ti, scalar=0.5, in1=rr, op0=ALU.mult, op1=ALU.mult))
                    for b in range(HC):
                        last = nc.vector.tensor_tensor_scan(rr[:, b, :], aa[:, b, :], ti[:, b, :], 0.0, ALU.mult, ALU.add)
                    link(last)
                    dve.wait_ge(turned_act, turn * 2 + 4)
                    nc.vector.tensor_tensor(ti, rr, xc, ALU.mult).then_inc(lru_y, 1)
                    split(gl, 9, 11)
                    dve.wait_ge(lru_y_hi, col + 1)
                    nc.vector.tensor_tensor(bufb_lo[:, ds(blk, HC), :], ti, bufb_hi[:, ds(blk, HC), :].bitcast(F32),
                                            ALU.subtract).then_inc(lru_y_lo, 1)
                    split(gl, 11, 12)
                chain.leave(COLS // 2)

            for b in range(TB):
                dve.wait_ge(acc_free[1][b], FREE + U_PLRU // 2)
            with dve.Fori(0, COLS // 2) as i:
                for n in range(2):
                    unit = (U_PLRU + n, i, 2)
                    split(unit, 4, 11)
                    acc_done(unit)
                    for b in range(TB):
                        part = merged[:, b, ds(n * NC + i * (2 * NC), NC)]
                        nc.vector.scalar_tensor_tensor(out=part, in0=part, scalar=1.0, in1=acc[pair(unit)][b][:, :],
                                                       op0=ALU.add, op1=ALU.mult).then_inc(acc_free[pair(unit)][b], 1)
                    split(unit, 11, 12)

            dve.wait_ge(iota_ready, 3)
            link(nc.vector.tensor_scalar(bits_i, dist_i, 3, None, ALU.bitwise_and))
            link(nc.vector.tensor_scalar(mask_a, bits_i, 0.0, None, ALU.is_equal))
            link(nc.vector.tensor_scalar(bits_i, dist_i, 15, None, ALU.bitwise_and))
            link(nc.vector.tensor_scalar(mask_b, bits_i, 0.0, None, ALU.is_equal))
            link(nc.vector.tensor_tensor(mask_a, mask_a, mask_b, ALU.add))
            link(nc.vector.tensor_copy(mask_c, dist_i))
            link(nc.vector.tensor_scalar(mask_b, mask_c, float(P), None, ALU.is_le))
            link(nc.vector.tensor_tensor(mask_a, mask_a, mask_b, ALU.add))
            link(nc.vector.tensor_scalar(mask_b, mask_c, 0.0, None, ALU.is_ge))
            link(nc.vector.tensor_tensor(count[:, :], mask_a, mask_b, ALU.mult))
            link(nc.vector.tensor_scalar(mask_b, count[:, :], 0.0, MASKED, ALU.is_equal, ALU.mult))
            nc.vector.tensor_tensor(dist[:, :], mask_b, mask_c, ALU.subtract).then_inc(masks_ready, 1)

            dve.wait_ge(slopes_ready, 1)
            dve.wait_ge(masks_ready, 1)
            with dve.Fori(0, COLS) as i:
                chain.enter(i, HC * 4)
                q, k, v, ga = ((U_ATT + n, i, 4) for n in range(4))
                turn = T_ATT + i * 2
                head = i * HC

                def bias_and_max(h):
                    dve.wait_ge(scores_done, FREE + head + h + 1)
                    dve.wait_ge(pt_done, FREE + head)
                    link(nc.vector.scalar_tensor_tensor(out=pr[:, h, :], in0=dist[:, :], scalar=slopes[:, ds(head + h, 1)],
                                                        in1=head_bank(h)[:, 0:3 * P], op0=ALU.mult, op1=ALU.add))
                    nc.vector.tensor_reduce(negmax[:, h, 0:1], pr[:, h, 0:P], AX_X, ALU.max)
                    link(nc.vector.tensor_reduce(negmax[:, h, 1:2], pr[:, h, P:3 * P], AX_X, ALU.max))
                    nc.vector.tensor_scalar(negmax[:, h, :], negmax[:, h, :], -1.0, None, ALU.mult).then_inc(max_ready, 1)

                def normalise(h):
                    dve.wait_ge(exp_done, head + h + 1)
                    for n, (lo, hi) in enumerate(((0, P), (P, 3 * P))):
                        last = nc.vector.scalar_tensor_tensor(out=pr[:, h, lo:hi], in0=pr[:, h, lo:hi], scalar=1.0,
                                                              in1=count[:, lo:hi], op0=ALU.mult, op1=ALU.mult,
                                                              accum_out=denom[:, h, n:n + 1])
                    link(last)
                    link(nc.vector.reciprocal(rdenom[:, h, :], denom[:, h, :]))
                    nc.vector.tensor_scalar(pr[:, h, 0:P], pr[:, h, 0:P], rdenom[:, h, 0:1], None, ALU.mult)
                    nc.vector.tensor_scalar(pr[:, h, P:3 * P], pr[:, h, P:3 * P], rdenom[:, h, 1:2], None,
                                            ALU.mult).then_inc(p_ready, 1)

                def y_rest(h):
                    dve.wait_ge(y_hi, head + h + 1)
                    nc.vector.tensor_tensor(bufb_lo[:, ds(head + h, 1), :], head_bank(h)[:, 0:SEQ].rearrange("p (k t) -> p k t", k=1),
                                            bufb_hi[:, ds(head + h, 1), :].bitcast(F32), ALU.subtract).then_inc(y_lo, 1)

                split(q, 4, 11)
                block_out(q, turn, 1)
                split(q, 11, 12)
                split(k, 4, 5)
                dve.wait_ge(scores_done, FREE + head)
                turn_copy(turn, q_t)
                split(k, 5, 11)
                block_out(k, turn + 1, 0)
                split(k, 11, 12)
                split(v, 4, 5)
                turn_copy(turn + 1, k_t)
                split(v, 5, 8)
                bias_and_max(0)
                split(v, 8, 9)
                bias_and_max(1)
                normalise(0)
                split(v, 9, 10)
                bias_and_max(2)
                normalise(1)
                split(v, 10, 11)
                bias_and_max(3)
                acc_done(v)
                dve.wait_ge(pv_done, FREE + head)
                nc.vector.tensor_scalar(v_n[:, 1, :], acc[pair(v)][1][:, :], rnorm[:, 0, 1:2], None,
                                        ALU.mult).then_inc(acc_free[pair(v)][1], 1)
                split(v, 11, 12)
                normalise(2)
                split(ga, 4, 5)
                normalise(3)
                split(ga, 5, 6)
                y_rest(0)
                split(ga, 6, 7)
                y_rest(1)
                split(ga, 7, 9)
                y_rest(2)
                split(ga, 9, 10)
                y_rest(3)
                split(ga, 10, 12)
                chain.leave(COLS)

            for b in range(TB):
                dve.wait_ge(acc_free[1][b], FREE + U_PATT // 2)
            for c in range(COLS):
                unit = (U_PATT + c, 0, 0)
                split(unit, 4, 5)
                if c:
                    turn_lo(T_MERGE + c - 1, bufa_lo, bufa_hi, HC * (c - 1), scale=0.5)
                split(unit, 5, 11)
                acc_done(unit)
                dve.wait_ge(pe_turned, 2 * (T_MERGE + c))
                for b in range(TB):
                    nc.vector.scalar_tensor_tensor(out=block_n[:, b, :], in0=gate_a[:, b, c * NC:(c + 1) * NC], scalar=1.0,
                                                   in1=acc[pair(unit)][b][:, :], op0=ALU.add,
                                                   op1=ALU.mult).then_inc(acc_free[pair(unit)][b], 1)
                for b in range(TB):
                    dve.wait_ge(acc_free[pair(unit)][b], read_out(unit))
                    last = nc.vector.tensor_tensor(block_n[:, b, :], block_n[:, b, :], merged[:, b, c * NC:(c + 1) * NC], ALU.add)
                last.then_inc(block_ready, 1)
                split(unit, 11, 12)

            def add_to_resid(unit, n):
                acc_done(unit)
                for b in range(TB):
                    part = resid[:, b, n * NC:(n + 1) * NC]
                    nc.vector.tensor_tensor(part, part, acc[pair(unit)][b][:, :], ALU.add).then_inc(acc_free[pair(unit)][b], 1)

            for c in range(COLS):
                unit = (U_OUT + c, 0, 0)
                split(unit, 4, 5)
                if c == 0:
                    turn_lo(T_H - 1, bufa_lo, bufa_hi, HC * (COLS - 1), scale=0.5)
                else:
                    turn_lo(T_H + c - 1, bufb_lo, bufb_hi, HC * (c - 1), gain=mlp_gain)
                split(unit, 5, 11)
                add_to_resid(unit, c)
                split(unit, 11, 12)

            def group(unit0, turn0, first=False, last=False):
                base, i, per = unit0
                for n in range(COLS):
                    unit = (base + n, i, per)
                    split(unit, 4, 5)
                    if n:
                        turn_lo(turn0 + (n - 1), bufa_lo, bufa_hi, HC * (n - 1))
                        split(unit, 5, 11)
                    elif first:
                        turn_lo(T_HID - 1, bufb_lo, bufb_hi, HC * (COLS - 1), gain=mlp_gain)
                        variance(TB + TB * COLS, sumsq[:, 1, :].rearrange("p (b c) -> p b c", c=COLS))
                        split(unit, 5, 8)
                        rsqrt(2, rnorm[:, 3, :]).then_inc(rnorm_ready, 1)
                        split(unit, 8, 11)
                    else:
                        split(unit, 5, 11)
                    for b in range(TB):
                        dve.wait_ge(acc_free[pair(unit)][b], read_out(unit))
                        last_sq = nc.vector.tensor_tensor(block_n[:, b, :], block_n[:, b, :], block_n[:, b, :], ALU.mult)
                    last_sq.then_inc(block_ready, 1)
                    split(unit, 11, 12)
                for n in range(COLS):
                    unit = (base + COLS + n, i, per)
                    split(unit, 4, 5)
                    if n == 0:
                        turn_lo(turn0 + (COLS - 1), bufa_lo, bufa_hi, HC * (COLS - 1))
                    ends = last and n == COLS - 1
                    split(unit, 5, 8 if ends else 11)
                    add_to_resid(unit, n)
                    if not ends:
                        split(unit, 11, 12)
                    if last:
                        dve.wait_ge(gf_landed, 16)
                        for b in range(TB):
                            dve.wait_ge(squares_ready, TB * (1 + COLS + n) + b + 1)
                            part = resid[:, b, n * NC:(n + 1) * NC]
                            last_gain = nc.vector.tensor_tensor(part, part, merged[:, 0, n * NC:(n + 1) * NC], ALU.mult)
                        last_gain.then_inc(gained, 1)

            mlp_groups(dve, group)

            variance(TB + 2 * TB * COLS, sumsq[:, 0, :].rearrange("p (b c) -> p b c", c=COLS))
            rsqrt(3, rnorm[:, 4, :]).then_inc(rnorm_ready, 1)
            dve.wait_ge(rnorm_ready, 3)
            dve.wait_ge(gained, COLS)
            for c in range(COLS):
                part = resid[:, 1, c * NC:(c + 1) * NC]
                nc.vector.tensor_scalar(part, part, rnorm[:, 4, 1:2], None, ALU.mult).then_inc(final_dve, 1)


_INS = ["x", "norm_mix_g", "w_in", "conv_w", "conv_b", "lru_wa", "lru_ba", "lru_wx", "lru_bx", "lru_lambda",
        "w_proj_attn", "w_proj_lru", "w_out", "norm_mlp_g", "w_up", "w_down", "norm_final_g"]


def kernel(**inputs):
    import numpy as _np
    import concourse.bacc as _bacc
    from concourse.bass_utils import run_bass_kernel_spmd as _run

    nc = _bacc.Bacc("TRN2", target_bir_lowering=False, num_devices=1)
    arrays, args = {}, []
    for name in _INS:
        a = _np.ascontiguousarray(inputs[name])
        arrays[f"in_{name}"] = a
        args.append(nc.dram_tensor(f"in_{name}", a.shape, mybir.dt.from_np(a.dtype), kind="ExternalInput").ap())
    args.append(nc.dram_tensor("out", (1, SEQ, D), F32, kind="ExternalOutput").ap())
    build(nc, *args)
    r = _run(nc, [arrays], core_ids=[0])
    return r.results[0]["out"]
```
